# Optimizing a Trainium2 kernel written in Bass

```python
import jax, jax.numpy as jnp
from jax import lax
import numpy as np

D_MODEL = 1024
BATCH = 1
SEQ = 1024
DEPTH = 1
DEC_BATCH = 1
DEC_SEQ = 32
PAST_LEN = 2048

CHUNK = 64
HEAD_DIM = 64
N_SB_HEADS = 8
N_SWA_HEADS = 8
N_SWA_KV_HEADS = 2
SWA_GROUP = N_SWA_HEADS // N_SWA_KV_HEADS
WINDOW = 128
N_BAND = WINDOW // CHUNK + 1
SB_BLOCK = 128
SB_WIDTH = N_SB_HEADS * HEAD_DIM
SWA_WIDTH = N_SWA_HEADS * HEAD_DIM
SWA_KV_WIDTH = N_SWA_KV_HEADS * HEAD_DIM
MIX_WIDTH = SB_WIDTH + SWA_WIDTH
IN_WIDTH = 3 * SB_WIDTH + SWA_WIDTH + 2 * SWA_KV_WIDTH
SPLITS = (SB_WIDTH, 2 * SB_WIDTH, 3 * SB_WIDTH, 3 * SB_WIDTH + SWA_WIDTH,
          3 * SB_WIDTH + SWA_WIDTH + SWA_KV_WIDTH)
N_KEYS = 128
N_EXPERTS = N_KEYS * N_KEYS
N_PEER_HEADS = 8
PEER_QUERY_DIM = 256
PEER_HALF = PEER_QUERY_DIM // 2
PEER_TOPK = 16
PEER_BLOCK = 128
RMS_EPS = 1e-6

kernel_name = 'stickbreak_swa_peer_streaming_step'

def rms_norm(x, g):
    xf = x.astype(jnp.float32)
    y = xf * lax.rsqrt(jnp.mean(xf * xf, axis=-1, keepdims=True) + RMS_EPS)
    return (y * g.astype(jnp.float32)).astype(x.dtype)

def alibi_slopes():
    h = np.arange(1, N_SWA_HEADS + 1, dtype=np.float32)
    slopes = (2.0 ** (-8.0 * h / N_SWA_HEADS)).astype(np.float32)
    return jnp.asarray(slopes).reshape(N_SWA_KV_HEADS, SWA_GROUP)

def project_heads(xn, w_in):
    b, t, _ = xn.shape
    p = xn @ w_in
    q_sb, k_sb, v_sb, q_sw, k_sw, v_sw = jnp.split(p, SPLITS, axis=-1)
    q_sb = q_sb.reshape(b, t, N_SB_HEADS, HEAD_DIM)
    k_sb = k_sb.reshape(b, t, N_SB_HEADS, HEAD_DIM)
    v_sb = v_sb.reshape(b, t, N_SB_HEADS, HEAD_DIM)
    q_sw = q_sw.reshape(b, t, N_SWA_KV_HEADS, SWA_GROUP, HEAD_DIM)
    k_sw = k_sw.reshape(b, t, N_SWA_KV_HEADS, HEAD_DIM)
    v_sw = v_sw.reshape(b, t, N_SWA_KV_HEADS, HEAD_DIM)
    return q_sb, k_sb, v_sb, q_sw, k_sw, v_sw

def stick_breaking(q, k, v, q_pos, k_pos):
    z = jnp.einsum('bqhd,bshd->bhqs', q, k).astype(jnp.float32) * (HEAD_DIM ** -0.5)
    visible = (k_pos[None, :] < q_pos[:, None])[None, None]
    log_keep = jnp.where(visible, jax.nn.log_sigmoid(-z), 0.0)
    between = lax.cumsum(log_keep, axis=3, reverse=True) - log_keep
    a = jnp.where(visible, jnp.exp(jax.nn.log_sigmoid(z) + between), 0.0)
    return jnp.einsum('bhqs,bshd->bqhd', a.astype(v.dtype), v)

def sb_prompt(q, k, v):
    s = q.shape[1]
    outs = []
    for i in range(s // SB_BLOCK):
        lo, hi = i * SB_BLOCK, (i + 1) * SB_BLOCK
        outs.append(stick_breaking(q[:, lo:hi], k[:, :hi], v[:, :hi],
                                   jnp.arange(lo, hi), jnp.arange(hi)))
    return jnp.concatenate(outs, axis=1)

def sink_window_attention(q, k, v, q_pos, k_pos, slopes, sinks):
    s = jnp.einsum('bnqkgd,bnskd->bnkgqs', q, k).astype(jnp.float32) * (HEAD_DIM ** -0.5)
    dist = jnp.abs(q_pos[:, :, None] - k_pos[:, None, :]).astype(jnp.float32)
    s = s - slopes[None, None, :, :, None, None] * dist[None, :, None, None, :, :]
    s = jnp.where((k_pos >= 0)[None, :, None, None, None, :], s, -jnp.inf)
    sink = sinks.astype(jnp.float32).reshape(N_SWA_KV_HEADS, SWA_GROUP)[None, None, :, :, None, None]
    m = jnp.maximum(jnp.max(s, axis=-1, keepdims=True), sink)
    p = jnp.exp(s - m)
    w = p / (jnp.sum(p, axis=-1, keepdims=True) + jnp.exp(sink - m))
    return jnp.einsum('bnkgqs,bnskd->bnqkgd', w.astype(v.dtype), v)

def swa_prompt(q, k, v, slopes, sinks):
    b, s = q.shape[:2]
    nc = s // CHUNK
    qc = q.reshape(b, nc, CHUNK, N_SWA_KV_HEADS, SWA_GROUP, HEAD_DIM)
    pad = ((0, 0), (WINDOW, 0), (0, 0), (0, 0))
    kc = jnp.pad(k, pad).reshape(b, nc + N_BAND - 1, CHUNK, N_SWA_KV_HEADS, HEAD_DIM)
    vc = jnp.pad(v, pad).reshape(b, nc + N_BAND - 1, CHUNK, N_SWA_KV_HEADS, HEAD_DIM)
    kb = jnp.concatenate([kc[:, j:j + nc] for j in range(N_BAND)], axis=2)
    vb = jnp.concatenate([vc[:, j:j + nc] for j in range(N_BAND)], axis=2)
    q_pos = jnp.arange(s).reshape(nc, CHUNK)
    k_pos = (jnp.arange(nc) * CHUNK)[:, None] - WINDOW + jnp.arange(N_BAND * CHUNK)[None, :]
    o = sink_window_attention(qc, kb, vb, q_pos, k_pos, slopes, sinks)
    return o.reshape(b, s, SWA_WIDTH)

def swa_sample(q, kb, vb, past, slopes, sinks):
    b, t = q.shape[:2]
    q_pos = past + jnp.arange(t)
    k_pos = past - WINDOW + jnp.arange(WINDOW + t)
    o = sink_window_attention(q[:, None], kb[:, None], vb[:, None], q_pos[None], k_pos[None], slopes, sinks)
    return o.reshape(b, t, SWA_WIDTH)

def peer_ffn(x, w_q, keys_1, keys_2, u, v):
    lead = x.shape[:-1]
    xt = x.reshape(-1, D_MODEL)
    t = xt.shape[0]
    q = (xt @ w_q).reshape(t, N_PEER_HEADS, 2, PEER_HALF)
    s1 = jnp.einsum('thd,nd->thn', q[:, :, 0], keys_1).astype(jnp.float32)
    s2 = jnp.einsum('thd,nd->thn', q[:, :, 1], keys_2).astype(jnp.float32)
    v1, i1 = lax.top_k(s1, PEER_TOPK)
    v2, i2 = lax.top_k(s2, PEER_TOPK)
    cand = (v1[..., :, None] + v2[..., None, :]).reshape(t, N_PEER_HEADS, PEER_TOPK * PEER_TOPK)
    cidx = (i1[..., :, None] * N_KEYS + i2[..., None, :]).reshape(t, N_PEER_HEADS, PEER_TOPK * PEER_TOPK)
    best, pos = lax.top_k(cand, PEER_TOPK)
    idx = jnp.take_along_axis(cidx, pos, axis=-1)
    gate = jax.nn.softmax(best, axis=-1).astype(x.dtype)
    npad = (-t) % PEER_BLOCK
    xb = jnp.pad(xt, ((0, npad), (0, 0))).reshape(-1, PEER_BLOCK, D_MODEL)
    ib = jnp.pad(idx, ((0, npad), (0, 0), (0, 0))).reshape(-1, PEER_BLOCK, N_PEER_HEADS, PEER_TOPK)
    gb = jnp.pad(gate, ((0, npad), (0, 0), (0, 0))).reshape(-1, PEER_BLOCK, N_PEER_HEADS, PEER_TOPK)

    def expert_block(args):
        xs, ids, gs = args
        hid = jax.nn.gelu(jnp.einsum('thkd,td->thk', u[ids], xs), approximate=False)
        return jnp.einsum('thk,thkd->td', gs * hid, v[ids])

    y = lax.map(expert_block, (xb, ib, gb)).reshape(-1, D_MODEL)[:t]
    return y.reshape(*lead, D_MODEL)

def block_tail(x, o_sb, o_sw, g_sb, g_sw, w_out, g_ffn, w_q, keys_1, keys_2, u, v):
    b, t = x.shape[:2]
    merged = jnp.concatenate([rms_norm(o_sb.reshape(b, t, SB_WIDTH), g_sb),
                              rms_norm(o_sw.reshape(b, t, SWA_WIDTH), g_sw)], axis=-1)
    h = x + merged @ w_out
    return h + peer_ffn(rms_norm(h, g_ffn), w_q, keys_1, keys_2, u, v)

def setup_inputs(seed: int = 0) -> dict:
    key = jax.random.key(seed)
    ks = jax.random.split(key, 20)

    def nrm(k, shape, scale):
        return jax.random.normal(k, shape, jnp.float32) * scale

    return {
        'x_prompt': nrm(ks[0], (BATCH, SEQ, D_MODEL), 1.0),
        'x_sample': nrm(ks[1], (DEC_BATCH, DEC_SEQ, D_MODEL), 1.0),
        'cache_sb_k': nrm(ks[2], (DEPTH, DEC_BATCH, PAST_LEN, N_SB_HEADS, HEAD_DIM), 1.0),
        'cache_sb_v': nrm(ks[3], (DEPTH, DEC_BATCH, PAST_LEN, N_SB_HEADS, HEAD_DIM), 1.0),
        'cache_swa_k': nrm(ks[4], (DEPTH, DEC_BATCH, WINDOW, N_SWA_KV_HEADS, HEAD_DIM), 1.0),
        'cache_swa_v': nrm(ks[5], (DEPTH, DEC_BATCH, WINDOW, N_SWA_KV_HEADS, HEAD_DIM), 1.0),
        'norm_mix': 1.0 + nrm(ks[6], (DEPTH, D_MODEL), 0.1),
        'w_in': nrm(ks[7], (DEPTH, D_MODEL, IN_WIDTH), D_MODEL ** -0.5),
        'swa_sinks': nrm(ks[8], (DEPTH, N_SWA_HEADS), 1.0),
        'norm_sb_out': 1.0 + nrm(ks[9], (DEPTH, SB_WIDTH), 0.1),
        'norm_swa_out': 1.0 + nrm(ks[10], (DEPTH, SWA_WIDTH), 0.1),
        'w_out': nrm(ks[11], (DEPTH, MIX_WIDTH, D_MODEL), MIX_WIDTH ** -0.5),
        'norm_ffn': 1.0 + nrm(ks[12], (DEPTH, D_MODEL), 0.1),
        'w_peer_q': nrm(ks[13], (DEPTH, D_MODEL, N_PEER_HEADS * PEER_QUERY_DIM), D_MODEL ** -0.5),
        'peer_keys_1': nrm(ks[14], (DEPTH, N_KEYS, PEER_HALF), PEER_HALF ** -0.5),
        'peer_keys_2': nrm(ks[15], (DEPTH, N_KEYS, PEER_HALF), PEER_HALF ** -0.5),
        'peer_u': nrm(ks[16], (DEPTH, N_EXPERTS, D_MODEL), D_MODEL ** -0.5),
        'peer_v': nrm(ks[17], (DEPTH, N_EXPERTS, D_MODEL), 0.5),
        'norm_final': 1.0 + nrm(ks[18], (D_MODEL,), 0.1),
    }

def reference(x_prompt, x_sample, cache_sb_k, cache_sb_v, cache_swa_k, cache_swa_v,
              norm_mix, w_in, swa_sinks, norm_sb_out, norm_swa_out, w_out, norm_ffn,
              w_peer_q, peer_keys_1, peer_keys_2, peer_u, peer_v, norm_final):
    slopes = alibi_slopes()
    past = cache_sb_k.shape[2]
    xp, xs = x_prompt, x_sample
    p_sb_k, p_sb_v, p_sw_k, p_sw_v = [], [], [], []
    s_sb_k, s_sb_v, s_sw_k, s_sw_v = [], [], [], []
    for l in range(DEPTH):
        q_sb, k_sb, v_sb, q_sw, k_sw, v_sw = project_heads(rms_norm(xp, norm_mix[l]), w_in[l])
        o_sb = sb_prompt(q_sb, k_sb, v_sb)
        o_sw = swa_prompt(q_sw, k_sw, v_sw, slopes, swa_sinks[l])
        xp = block_tail(xp, o_sb, o_sw, norm_sb_out[l], norm_swa_out[l], w_out[l], norm_ffn[l],
                        w_peer_q[l], peer_keys_1[l], peer_keys_2[l], peer_u[l], peer_v[l])
        p_sb_k.append(k_sb)
        p_sb_v.append(v_sb)
        p_sw_k.append(k_sw[:, -WINDOW:])
        p_sw_v.append(v_sw[:, -WINDOW:])
        t = xs.shape[1]
        q_sb, k_sb, v_sb, q_sw, k_sw, v_sw = project_heads(rms_norm(xs, norm_mix[l]), w_in[l])
        k_all = jnp.concatenate([cache_sb_k[l], k_sb], axis=1)
        v_all = jnp.concatenate([cache_sb_v[l], v_sb], axis=1)
        o_sb = stick_breaking(q_sb, k_all, v_all, past + jnp.arange(t), jnp.arange(past + t))
        kw = jnp.concatenate([cache_swa_k[l], k_sw], axis=1)
        vw = jnp.concatenate([cache_swa_v[l], v_sw], axis=1)
        o_sw = swa_sample(q_sw, kw, vw, past, slopes, swa_sinks[l])
        xs = block_tail(xs, o_sb, o_sw, norm_sb_out[l], norm_swa_out[l], w_out[l], norm_ffn[l],
                        w_peer_q[l], peer_keys_1[l], peer_keys_2[l], peer_u[l], peer_v[l])
        s_sb_k.append(k_sb)
        s_sb_v.append(v_sb)
        s_sw_k.append(kw[:, -WINDOW:])
        s_sw_v.append(vw[:, -WINDOW:])
    y_prompt = rms_norm(xp, norm_final)
    y_sample = rms_norm(xs, norm_final)
    return (y_prompt, y_sample,
            jnp.stack(p_sb_k), jnp.stack(p_sb_v), jnp.stack(p_sw_k), jnp.stack(p_sw_v),
            jnp.stack(s_sb_k), jnp.stack(s_sb_v), jnp.stack(s_sw_k), jnp.stack(s_sw_v))


_drawn_inputs = setup_inputs


def setup_inputs(seed=0):
    import zlib

    import numpy as np

    out = dict(_drawn_inputs(seed))
    spreads = {}
    factors = {}
    for name, (base, spread) in spreads.items():
        noise = np.random.default_rng([zlib.crc32(name.encode()), seed]).standard_normal(out[name].shape)
        drawn = base * np.exp(spread * noise) if base else spread * noise
        out[name] = __import__('jax').numpy.asarray(drawn.astype(out[name].dtype))
    for name, factor in factors.items():
        out[name] = (out[name] * factor).astype(out[name].dtype)
    return out
```

```python
from contextlib import ExitStack

import numpy as np

import concourse.bass as bass
from concourse import mybir

ALU = mybir.AluOpType
ACT = mybir.ActivationFunctionType
AXX = mybir.AxisListType.X
F32 = mybir.dt.float32
U32 = mybir.dt.uint32

P = 128
DM = 1024
DK = DM // P
SEQ = 1024
NT = SEQ // P
TS = 32
TOK = SEQ + TS
PAST = 2048
HD = 64
NH = 8
SBW = NH * HD
WIN = 128
CHUNK = 64
KVW = 2 * HD
INW = 3 * SBW + SBW + 2 * KVW
C_QSB, C_KV, C_QSW, C_KVSW, C_END = 0, 4, 12, 16, 18
NATW = 2 * SBW + 2 * KVW
PH = 8
TOPK = 16
NKEY = 128
QH = 128
EPS = 1e-6
SCALE = HD ** -0.5
MASKED = -1e30
LOWEST = -3.0e38
PAIR_ROWS = [(a, TOPK // (a + 1)) for a in range(TOPK)]
NCAND = sum(n for _, n in PAIR_ROWS)
RING = 8
SLOTS = PH * TOPK
COPIES = P // TS
PART = TOPK // COPIES


def constants():
    s = np.arange(P)
    suffix = (s[:, None] >= s[None, :]).astype(np.float32)
    before = (s[:, None] < s[None, :]).astype(np.float32)
    c = {
        "ident": np.eye(P, dtype=np.float32),
        "neg_suffix": -suffix,
        "neg_ones": -np.ones((P, P), np.float32),
        "visible": before,
        "hidden": np.tile((1 - before) * np.float32(MASKED), (1, 4)).astype(np.float32),
        "rank_iota": np.tile(np.arange(NCAND, dtype=np.float32), (P, 1)),
    }
    slopes = (2.0 ** (-8.0 * np.arange(1, NH + 1, dtype=np.float32) / NH)).astype(np.float32)
    q, k = np.arange(P), np.arange(2 * P) - P
    dist = np.abs(q[:, None] - k[None, :]).astype(np.float32)
    lo = (q // CHUNK) * CHUNK - WIN
    seen = (k[None, :] >= lo[:, None]) & (k[None, :] < lo[:, None] + WIN + CHUNK)
    bias = np.where(seen[:, None, :], -slopes[None, :, None] * dist[:, None, :], MASKED)
    first = np.where((k >= 0)[None, None, :], bias, MASKED)
    c["alibi"] = np.stack([first, bias]).astype(np.float32).reshape(2, P, NH * 2 * P)
    qs, ks = np.arange(TS), np.arange(WIN + TS) - WIN
    dist = np.abs(qs[:, None] - ks[None, :]).astype(np.float32)
    c["fold"] = np.tile(np.eye(TS, dtype=np.float32), (P // TS, 1))
    c["alibi_sample"] = (-slopes[None, :, None] * dist[:, None, :]).astype(np.float32).reshape(TS, -1)
    return c


def rsqrt_guess(nc, act, mean, work, out):
    nc.scalar.activation(work, mean, ACT.Ln)
    act.drain()
    return nc.scalar.activation(out, work, ACT.Exp, scale=-0.5)


def rsqrt_newton(nc, dve, mean, guess, work, out):
    nc.vector.tensor_tensor(work, guess, guess, ALU.mult)
    dve.drain()
    nc.vector.tensor_tensor(work, work, mean, ALU.mult)
    dve.drain()
    nc.vector.tensor_scalar(work, work, -0.5, 1.5, ALU.mult, ALU.add)
    dve.drain()
    return nc.vector.tensor_tensor(out, work, guess, ALU.mult)


def hold(engine, sem, value):
    engine.wait_ge(sem, value)
    engine.nop(nofuse=True)


def tile_index(nc, j):
    if isinstance(j, int):
        return j
    return nc.s_assert_within(j, 0, NT - 1, skip_runtime_bounds_check_because="back runs below t")


def projection_phase(nc, io):
    with ExitStack() as ctx:
        sb = lambda name, shape: ctx.enter_context(nc.sbuf_tensor(name, shape, F32))
        ps = lambda name, shape: ctx.enter_context(nc.psum_tensor(name, shape, F32))
        sem = lambda name: ctx.enter_context(nc.semaphore(name))

        ident = sb("p1_ident", [P, P])
        g_mix = sb("g_mix", [P, DK])
        x_in = sb("x_in", [P, 2, DM])
        squares = sb("squares", [P, 2, DM])
        stat = sb("p1_stat", [P, 2, 6])
        xnT = sb("xnT", [P, DK, TOK])
        w = sb("w_cols", [P, 2, DK, P])
        stage = sb("stage", [P, 2, TOK])
        nat = sb("nat", [P, 2, NT + 1, P])
        acc = [ps(f"proj{s}", [P, 3 * 512]) for s in range(2)]
        turn = ps("turn", [P, 2 * 512])

        s_const = sem("p1_const")
        s_x = [sem(f"x_loaded{s}") for s in range(2)]
        s_sq = sem("squares_summed")
        s_mean = sem("mean_ready")
        s_guess = sem("guess_ready")
        s_xs = sem("x_scaled")
        s_xT = sem("x_turned")
        s_xnT = sem("xnT_free")
        s_w = [sem(f"w_loaded{s}") for s in range(2)]
        s_mm = sem("projected")
        s_evA = sem("stage_by_act")
        s_evD = sem("stage_by_dve")
        s_st = [sem(f"stage_stored{s}") for s in range(2)]
        s_tr = sem("natural_turned")
        s_nat = sem("natural_ready")
        s_ns = [sem(f"natural_stored{s}") for s in range(2)]
        block = ctx.enter_context(nc.Block())

        def tiles(engine, step):
            with engine.Fori(0, NT // 2) as pair:
                for s in range(2):
                    step(pair * 2 + s, s, pair, P)
            step(NT, 0, NT // 2, TS)

        def columns(engine, steps):
            for lo, hi, kv0 in ((C_QSB, C_KV, None), (C_KV, C_QSW, 0), (C_QSW, C_KVSW, None),
                                (C_KVSW, C_END, C_QSW - C_KV)):
                def run(pair):
                    for step in steps:
                        for s in range(2):
                            kv = None if kv0 is None else pair * 2 + (s + kv0 - lo)
                            step(pair * 2 + s, s, pair, kv, lo)
                run(lo // 2)
                if hi - lo > 2:
                    with engine.Fori(lo // 2 + 1, hi // 2) as pair:
                        run(pair)

        @block.sync
        def _(sp):
            sp.dma_start(ident[:], io["ident"]).then_inc(s_const, 16)
            sp.dma_start(g_mix[:], io["norm_mix"].rearrange("o (k p) -> p (o k)", p=P),
                         allow_slow_non_contiguous=True).then_inc(s_const, 16)

            def load_x(t, s, pair, rows):
                sp.wait_ge(s_xnT, t + 1)
                src = io["x_prompt"][bass.ds(t * P, P), :] if rows == P else io["x_sample"]
                sp.dma_start(x_in[0:rows, s, :], src).then_inc(s_x[s], 16)
            tiles(sp, load_x)

            def load_w(c, s):
                src = io["w_in"].rearrange("(k p) n -> p k n", p=P)[:, :, bass.ds(c * P, P)]
                sp.dma_start(w[:, s, :, :], src).then_inc(s_w[s], 16)
            load_w(0, 0)
            load_w(1, 1)
            with sp.Fori(0, C_END // 2 - 1) as pair:
                for s in range(2):
                    sp.wait_ge(s_mm, pair * 2 + (s + 1))
                    load_w(pair * 2 + (s + 2), s)

        @block.scalar
        def _(act):
            act.preload_act_table_set("natural_log_exp_and_others")

            def square(t, s, pair, rows):
                act.wait_ge(s_x[s], (pair + 1) * 16)
                nc.scalar.activation(squares[0:rows, s, :], x_in[0:rows, s, :], ACT.Square,
                                     accum_out=stat[0:rows, s, 0:1]).then_inc(s_sq, 1)
                act.wait_ge(s_mean, t + 1)
                rsqrt_guess(nc, act, stat[0:rows, s, 1:2], stat[0:rows, s, 2:3],
                            stat[0:rows, s, 3:4]).then_inc(s_guess, 1)
            tiles(act, square)

            act.sem_inc(s_evA, 2)

            def evacuate(c, s, pair, kv, lo):
                act.wait_ge(s_mm, c + 1)
                act.wait_ge(s_st[s], pair * 16)
                act.wait_ge(s_tr, {C_QSB: 2, C_QSW: 10, C_KVSW: 10}[lo] if kv is None or lo == C_KVSW else kv + 1)
                scale = SCALE if kv is None else 1.0
                nc.scalar.activation(stage[:, s, 0:512], acc[s][:, 0:512], ACT.Copy, scale=scale)
                nc.scalar.activation(stage[:, s, SEQ:TOK], acc[s][:, 1024:1024 + TS], ACT.Copy,
                                     scale=scale).then_inc(s_evA, 1)
            columns(act, [evacuate])

        @block.vector
        def _(dve):
            dve.sem_inc(s_xnT, 2)
            dve.wait_ge(s_const, 32)

            def normalise(t, s, pair, rows):
                dve.wait_ge(s_sq, t + 1)
                nc.vector.tensor_scalar(stat[0:rows, s, 1:2], stat[0:rows, s, 0:1], 1.0 / DM, EPS,
                                        ALU.mult, ALU.add).then_inc(s_mean, 1)
                dve.wait_ge(s_guess, t + 1)
                rsqrt_newton(nc, dve, stat[0:rows, s, 1:2], stat[0:rows, s, 3:4], stat[0:rows, s, 4:5],
                             stat[0:rows, s, 5:6])
                dve.drain()
                nc.vector.tensor_scalar(x_in[0:rows, s, :], x_in[0:rows, s, :], stat[0:rows, s, 5:6],
                                        None, ALU.mult).then_inc(s_xs, 1)
                dve.wait_ge(s_xT, t + 1)
                out = xnT[:, :, bass.ds(t * P, P)] if rows == P else xnT[:, :, SEQ:TOK]
                src = acc[s][:, 0:DM].rearrange("p (k t) -> p k t", k=DK)[:, :, 0:rows]
                nc.vector.tensor_tensor(out, src, g_mix[:].unsqueeze(2).broadcast_to([P, DK, rows]),
                                        ALU.mult).then_inc(s_xnT, 1)
            tiles(dve, normalise)

            dve.sem_inc(s_evD, 2)

            def evacuate(c, s, pair, kv, lo):
                dve.wait_ge(s_mm, c + 1)
                dve.wait_ge(s_st[s], pair * 16)
                dve.wait_ge(s_tr, {C_QSB: 2, C_QSW: 10, C_KVSW: 10}[lo] if kv is None or lo == C_KVSW else kv + 1)
                nc.vector.tensor_scalar(stage[:, s, 512:1024], acc[s][:, 512:1024],
                                        SCALE if kv is None else 1.0, None, ALU.mult).then_inc(s_evD, 1)

            def natural(c, s, pair, kv, lo):
                if kv is None:
                    return
                dve.wait_ge(s_tr, kv + 3)
                dve.wait_ge(s_ns[s], (pair - lo // 2) * 32 if lo == C_KV else (C_QSW - C_KV) // 2 * 32)
                nc.vector.tensor_copy(nat[:, s, 0:NT, :], turn[:].rearrange("p (t n) -> p t n", t=NT))
                nc.vector.tensor_copy(nat[0:TS, s, NT, :], acc[s][0:TS, 1152:1280]).then_inc(s_nat, 1)
            columns(dve, [evacuate, natural])

        @block.tensor
        def _(pe):
            pe.wait_ge(s_const, 32)

            def turn_x(t, s, pair, rows):
                pe.wait_ge(s_xs, t + 1)
                pe.wait_ge(s_xnT, t + 1)
                for k in range(DK):
                    last = nc.tensor.transpose(acc[s][:, k * P:k * P + rows], x_in[0:rows, s, k * P:(k + 1) * P],
                                               ident[0:rows, 0:rows])
                last.then_inc(s_xT, 1)
            tiles(pe, turn_x)

            pe.sem_inc(s_tr, 2)
            pe.wait_ge(s_xnT, 2 + NT + 1)

            def project(c, s, pair, kv, lo):
                pe.wait_ge(s_w[s], (pair + 1) * 16)
                pe.wait_ge(s_evA, c + 1)
                pe.wait_ge(s_evD, c + 1)
                if kv is None or lo == C_KVSW:
                    if lo != C_QSB:
                        pe.wait_ge(s_nat, C_QSW - C_KV)
                elif s == 1:
                    pe.wait_ge(s_nat, kv - 1)
                for a, b in ((0, 512), (512, 1024), (SEQ, TOK)):
                    for k in range(DK):
                        last = nc.tensor.matmul(acc[s][:, a:b], w[:, s, k, :], xnT[:, k, a:b],
                                                start=(k == 0), stop=(k == DK - 1))
                last.then_inc(s_mm, 1)

            def turn_natural(c, s, pair, kv, lo):
                if kv is None:
                    return
                pe.wait_ge(s_evA, c + 3)
                pe.wait_ge(s_evD, c + 3)
                pe.wait_ge(s_nat, kv)
                for t in range(NT):
                    nc.tensor.transpose(turn[:, t * P:(t + 1) * P], stage[:, s, t * P:(t + 1) * P], ident[:])
                nc.tensor.transpose(acc[s][0:TS, 1152:1280], stage[:, s, SEQ:TOK], ident[:]).then_inc(s_tr, 1)
            columns(pe, [project, turn_natural])

        @block.gpsimd
        def _(pool):
            def store(c, s, pair, kv, lo):
                pool.wait_ge(s_evA, c + 3)
                pool.wait_ge(s_evD, c + 3)
                pool.dma_start(io["projT"][c, :, :], stage[:, s, :]).then_inc(s_st[s], 16)

            def store_natural(c, s, pair, kv, lo):
                if kv is None:
                    return
                pool.wait_ge(s_nat, kv + 1)
                col = bass.ds(kv * P, P)
                pool.dma_start(io["nat"][0:SEQ, col].rearrange("(t p) n -> p t n", p=P),
                               nat[:, s, 0:NT, :]).then_inc(s_ns[s], 16)
                pool.dma_start(io["nat"][SEQ:TOK, col], nat[0:TS, s, NT, :]).then_inc(s_ns[s], 16)
            columns(pool, [store, store_natural])
            for s in range(2):
                pool.wait_ge(s_st[s], C_END // 2 * 16)
                pool.wait_ge(s_ns[s], NATW // P // 2 * 32)


def attention_phase(nc, io):
    with ExitStack() as ctx:
        sb = lambda name, shape: ctx.enter_context(nc.sbuf_tensor("at_" + name, shape, F32))
        ps = lambda name, shape: ctx.enter_context(nc.psum_tensor("at_" + name, shape, F32))
        sem = lambda name: ctx.enter_context(nc.semaphore(name))

        ident = sb("ident", [P, P])
        neg_suffix = sb("neg_suffix_sb", [P, P])
        neg_ones = sb("neg_ones_sb", [P, P])
        visible = sb("visible_sb", [P, P])
        hidden = sb("hidden_sb", [P, 4 * P])
        alibi = sb("alibi_sb", [P, NH, 2 * P])
        alibi_s = sb("alibi_s", [TS, NH, WIN + TS])
        sinks = sb("sinks", [P, NH])
        g_out = sb("g_out", [P, DK])
        g_ffn = sb("g_ffn", [P, DM])
        w_out = sb("w_out_sb", [P, DK, DM])
        q_pad = sb("q_pad", [P, 4, 2, P])
        kT = sb("kT", [P, 4, P])
        v_blk = sb("v_blk", [P, SBW])
        soft = sb("soft", [P, DM])
        sp = sb("sp", [P, DM])
        later = sb("later", [P, DM])
        probs = sb("probs", [P, DM])
        qw_pad = sb("qw_pad", [P, 4, 2, P])
        kw = sb("kw", [P, 2, 2 * P])
        vw = sb("vw", [P, 2, P])
        win_s = sb("win_s", [P, 4, 2 * P])
        win_pT = sb("win_pT", [P, DK, P])
        win = sb("win_stat", [P, 6, 4])
        rden = sb("rden", [P, NH])
        merged = sb("merged", [P, DM])
        mergedT = sb("mergedT", [P, DK, P])
        x_res = sb("x_res", [P, DM])
        h = sb("h_sb", [P, DM])
        xn = sb("xn_sb", [P, DM])
        xnT = sb("xnT_sb", [P, DK, P])
        junk = sb("junk", [P, DM])
        stat = sb("tail_stat", [P, 6, 2])
        qs_pad = sb("qs_pad", [P, 4, 2, TS])
        ksT = sb("ksT", [P, 4, TS])
        vs_blk = sb("vs_blk", [TS, SBW])
        cache_k = sb("cache_k", [P, 4, SBW])
        cache_v = sb("cache_v", [P, 4, SBW])
        cache_kT = sb("cache_kT", [P, 4, 4, P])
        qws_pad = sb("qws_pad", [P, 4, 2, TS])
        kws_in = sb("kws_in", [P, 2, 2, HD])
        kws = sb("kws", [P, 2, WIN + TS])
        vws = sb("vws", [P, 2, P])

        z = ps("z", [P, 4 * 512])
        o_sb = ps("o_sb", [P, 512])
        wide = ps("wide", [P, 1024])
        o_sw = ps("o_sw", [P, 512])

        names = """const zeroed q qs_in k v vs_in ks_in z ln sp tri a pv sw_in bias
                   zs nm p tp pTe pvw msw ssq mean2 guess2 mA mB tm mTe op h ssh meanh guessh
                   xn tx xTe x_in h_out xn_out xT_out
                   ck cv tk ckT cz cln csp ctri ca cpv kws_turn kws_copied copies""".split()
        S = {n: sem("a_" + n) for n in names}
        block = ctx.enter_context(nc.Block())

        def tiles(engine, step):
            step(0, True)
            with engine.Fori(1, NT) as t:
                step(t, False)

        def key_blocks(engine, t, first, n, diagonal, earlier):
            def one(step, j):
                step(engine.snap(n), t, j)
                engine.reg_add(n, n, 1)
            one(diagonal, t)
            if not first:
                with engine.Fori(0, t) as back:
                    one(earlier, t - 1 - back)

        def counter(engine):
            n = engine.alloc_register("pairs_" + str(engine.engine).split(".")[-1])
            engine.reg_mov(n, 0)
            return n

        @block.sync
        def _(sync):
            loads = ((ident[:], io["ident"]), (neg_suffix[:], io["neg_suffix"]), (neg_ones[:], io["neg_ones"]),
                     (visible[:], io["visible"]), (hidden[:], io["hidden"]),
                     (alibi[:].rearrange("p h k -> p (h k)"), io["alibi"][0]),
                     (alibi_s[:].rearrange("p h k -> p (h k)"), io["alibi_sample"]),
                     (sinks[:], io["swa_sinks"].partition_broadcast(P)),
                     (g_ffn[:], io["norm_ffn"].partition_broadcast(P)),
                     (w_out[:], io["w_out"].rearrange("(k p) n -> p k n", p=P)))
            for dst, src in loads:
                sync.dma_start(dst, src).then_inc(S["const"], 16)
            for k0, g in ((0, "norm_sb_out"), (4, "norm_swa_out")):
                sync.dma_start(g_out[:, k0:k0 + 4], io[g].rearrange("o (k p) -> p (o k)", p=P),
                               allow_slow_non_contiguous=True).then_inc(S["const"], 16)
            sync.wait_ge(S["zeroed"], 4)
            n = counter(sync)

            def load_k(n, t, j):
                hold(sync, S["z"], n + 1)
                j = tile_index(nc, j)
                src = io["projT"][4:8, :, bass.ds(j * P, P)].rearrange("c p t -> p c t")
                sync.dma_start(kT[:], src).then_inc(S["k"], 16)

            def tile(t, first):
                hold(sync, S["z"], sync.snap(n) + 1)
                for half in range(2):
                    rows = slice(half * HD, (half + 1) * HD)
                    src = io["projT"][0:4, rows, bass.ds(t * P, P)].rearrange("c p t -> p c t")
                    sync.dma_start(q_pad[rows, :, half, :], src).then_inc(S["q"], 16)
                hold(sync, S["q"], (t + 1) * 32)
                key_blocks(sync, t, first, n, load_k, load_k)
            tiles(sync, tile)
            load_k(sync.snap(n), 0, 0)

            def group(g):
                base = (3 - g) * 512
                hold(sync, S["ckT"], g * 2)
                sync.dma_start(cache_k[:], io["cache_sb_k"][bass.ds(base, 512), :].rearrange(
                    "(b s) c -> s b c", s=P)).then_inc(S["ck"], 16)
                hold(sync, S["cpv"], g + 1)
                sync.dma_start(cache_v[:], io["cache_sb_v"][bass.ds(base, 512), :].rearrange(
                    "(b s) c -> s b c", s=P)).then_inc(S["cv"], 16)
            group(0)
            with sync.Fori(1, 4) as g:
                group(g)

            nat = io["nat"]
            c2 = lambda name: io[name].rearrange("a b s n d -> (a b s) (n d)")
            for dst, src in (
                (c2("sb_k_prompt"), nat[0:SEQ, 0:SBW]), (c2("sb_v_prompt"), nat[0:SEQ, SBW:2 * SBW]),
                (c2("swa_k_prompt"), nat[SEQ - WIN:SEQ, 1024:1152]),
                (c2("swa_v_prompt"), nat[SEQ - WIN:SEQ, 1152:1280]),
                (c2("sb_k_sample"), nat[SEQ:TOK, 0:SBW]), (c2("sb_v_sample"), nat[SEQ:TOK, SBW:2 * SBW]),
                (c2("swa_k_sample")[0:WIN - TS], io["cache_swa_k"][TS:WIN, :]),
                (c2("swa_v_sample")[0:WIN - TS], io["cache_swa_v"][TS:WIN, :]),
                (c2("swa_k_sample")[WIN - TS:WIN], nat[SEQ:TOK, 1024:1152]),
                (c2("swa_v_sample")[WIN - TS:WIN], nat[SEQ:TOK, 1152:1280]),
            ):
                sync.dma_start(dst, src).then_inc(S["copies"], 16)
            sync.wait_ge(S["copies"], 160)

        @block.gpsimd
        def _(pool):
            for t in (q_pad, qw_pad, qs_pad, qws_pad):
                nc.gpsimd.memset(t[:], 0.0).then_inc(S["zeroed"], 1)
            hold(pool, S["zeroed"], 4)
            n = counter(pool)

            def load_v(n, t, j):
                hold(pool, S["pv"], n + 1)
                j = tile_index(nc, j)
                pool.dma_start(v_blk[:], io["nat"][bass.ds(j * P, P), SBW:2 * SBW]).then_inc(S["v"], 16)

            def load_halves(dst, c, t0, n_tok, sem):
                for half in range(2):
                    rows = slice(half * HD, (half + 1) * HD)
                    pool.dma_start(dst[rows, :, half, :], io["projT"][c:c + 4, rows, bass.ds(t0, n_tok)].rearrange(
                        "c p t -> p c t")).then_inc(sem, 16)

            def load_kw(dst, col, t0, n_tok, sem):
                for half in range(2):
                    rows = slice(half * HD, (half + 1) * HD)
                    pool.dma_start(dst[rows, :, col:col + n_tok], io["projT"][C_KVSW, :, bass.ds(t0, n_tok)].rearrange(
                        "(n d) t -> d n t", d=HD)).then_inc(sem, 16)

            def stores(t, rows, tokens):
                hold(pool, S["h"], t + 1)
                pool.dma_start(io["h"][tokens, :], h[0:rows, :]).then_inc(S["h_out"], 16)
                hold(pool, S["xn"], t + 1)
                pool.dma_start(io["xn2"][tokens, :], xn[0:rows, :]).then_inc(S["xn_out"], 16)
                hold(pool, S["xTe"], t + 1)
                pool.dma_start(io["xn2T"][t, :, :], xnT[:].rearrange("p k t -> p (k t)")).then_inc(S["xT_out"], 16)

            def tile(t, first):
                hold(pool, S["zs"], t * 2)
                load_halves(qw_pad, C_QSW, t * P, P, S["sw_in"])
                if first:
                    load_kw(kw, 0, 0, P, S["sw_in"])
                    load_kw(kw, P, 0, P, S["sw_in"])
                else:
                    load_kw(kw, 0, t * P - P, 2 * P, S["sw_in"])
                hold(pool, S["pvw"], t * 2)
                for b in range(2):
                    row = t * P + (b - 1) * P if not (first and b == 0) else 0
                    pool.dma_start(vw[:, b, :], io["nat"][bass.ds(row, P), 1152:1280]).then_inc(S["sw_in"], 16)
                hold(pool, S["h"], t)
                pool.dma_start(x_res[:], io["x_prompt"][bass.ds(t * P, P), :]).then_inc(S["x_in"], 16)
                key_blocks(pool, t, first, n, load_v, load_v)
                if first:
                    hold(pool, S["nm"], 2)
                    pool.dma_start(alibi[:].rearrange("p h k -> p (h k)"), io["alibi"][1]).then_inc(S["bias"], 16)
                stores(t, P, bass.ds(t * P, P))
            tiles(pool, tile)

            load_halves(qs_pad, 0, SEQ, TS, S["qs_in"])
            pool.dma_start(ksT[:], io["projT"][4:8, :, SEQ:TOK].rearrange("c p t -> p c t")).then_inc(S["qs_in"], 16)
            pool.dma_start(vs_blk[:], io["nat"][SEQ:TOK, SBW:2 * SBW]).then_inc(S["qs_in"], 16)
            load_halves(qws_pad, C_QSW, SEQ, TS, S["qs_in"])
            for twice in range(2):
                pool.dma_start(kws_in[:, :, twice, :], io["cache_swa_k"].rearrange(
                    "s (n d) -> s n d", n=2)).then_inc(S["qs_in"], 16)
            load_kw(kws, WIN, SEQ, TS, S["qs_in"])
            pool.dma_start(vws[:, 0, :], io["cache_swa_v"]).then_inc(S["qs_in"], 16)
            pool.dma_start(vws[0:TS, 1, :], io["nat"][SEQ:TOK, 1152:1280]).then_inc(S["qs_in"], 16)
            hold(pool, S["h"], NT)
            pool.dma_start(x_res[0:TS, :], io["x_sample"]).then_inc(S["x_in"], 16)
            stores(NT, TS, slice(SEQ, TOK))
            for name in ("h_out", "xn_out", "xT_out"):
                hold(pool, S[name], (NT + 1) * 16)
        N_QS = 12

        @block.scalar
        def _(act):
            act.preload_act_table_set("natural_log_exp_and_others")
            n = counter(act)

            def softplus_part(src, ready, ready_n, done):
                hold(act, ready, ready_n)
                nc.scalar.activation(soft[0:src.shape[0], 0:src.shape[1]], src, ACT.Abs)
                act.drain()
                view = soft[0:src.shape[0], 0:src.shape[1]]
                nc.scalar.activation(view, view, ACT.Exp, scale=-1.0)
                act.drain()
                nc.scalar.activation(view, view, ACT.Ln, bias=1.0).then_inc(done, 1)

            def pair(n, t, j):
                view = z[:, bass.ds((n % 2) * 1024, 1024)]
                softplus_part(view, S["z"], n + 2, S["ln"])
                act.wait_ge(S["tri"], n + 2)
                hold(act, S["pv"], n + 1)
                nc.scalar.activation(probs[:], view, ACT.Exp).then_inc(S["a"], 1)

            def window(u, f, rows, keys):
                act.wait_ge(S["nm"], u + 1)
                for hh in range(4):
                    nc.scalar.activation(win_s[0:rows, hh, 0:keys], win_s[0:rows, hh, 0:keys], ACT.Exp,
                                         bias=win[0:rows, 2, hh:hh + 1], accum_out=win[0:rows, 4, hh:hh + 1])
                nc.scalar.activation(win[0:rows, 5, :], win[0:rows, 3, :], ACT.Exp).then_inc(S["p"], 1)
                act.wait_ge(S["tp"], u + 1)
                act.wait_ge(S["pvw"], u)
                turned = wide[:].rearrange("p (k t) -> p k t", k=DK)
                if rows == P:
                    nc.scalar.activation(win_pT[:], turned, ACT.Copy).then_inc(S["pTe"], 1)
                else:
                    nc.scalar.activation(win_pT[:, 0:DK:2, 0:rows], turned[:, 0:DK:2, 0:rows], ACT.Copy)
                    nc.scalar.activation(win_pT[0:TS, 1:DK:2, 0:rows], turned[0:TS, 1:DK:2, 0:rows],
                                         ACT.Copy).then_inc(S["pTe"], 1)

            def tail(t, rows):
                act.wait_ge(S["msw"], t + 1)
                nc.scalar.activation(junk[0:rows, 0:512], o_sb[0:rows, :], ACT.Square, accum_out=stat[0:rows, 0, 0:1])
                nc.scalar.activation(junk[0:rows, 512:1024], merged[0:rows, 512:1024], ACT.Square,
                                     accum_out=stat[0:rows, 0, 1:2]).then_inc(S["ssq"], 1)
                act.wait_ge(S["mean2"], t + 1)
                rsqrt_guess(nc, act, stat[0:rows, 1, :], stat[0:rows, 2, :], stat[0:rows, 3, :]).then_inc(S["guess2"], 1)
                act.wait_ge(S["mB"], t + 1)
                nc.scalar.activation(merged[0:rows, 0:512], o_sb[0:rows, :], ACT.Copy,
                                     scale=stat[0:rows, 5, 0:1]).then_inc(S["mA"], 1)
                act.wait_ge(S["h"], t + 1)
                nc.scalar.activation(junk[0:rows, :], h[0:rows, :], ACT.Square,
                                     accum_out=stat[0:rows, 0, 0:1]).then_inc(S["ssh"], 1)
                act.wait_ge(S["meanh"], t + 1)
                rsqrt_guess(nc, act, stat[0:rows, 1, 0:1], stat[0:rows, 2, 0:1],
                            stat[0:rows, 3, 0:1]).then_inc(S["guessh"], 1)
                act.wait_ge(S["tx"], t + 1)
                act.wait_ge(S["xT_out"], t * 16)
                turned = wide[:].rearrange("p (k t) -> p k t", k=DK)[:, :, 0:rows]
                if rows == P:
                    nc.scalar.activation(xnT[:], turned, ACT.Copy).then_inc(S["xTe"], 1)
                else:
                    nc.scalar.activation(xnT[:].rearrange("p k (c t) -> p k c t", c=COPIES),
                                         turned.unsqueeze(2).broadcast_to([P, DK, COPIES, TS]),
                                         ACT.Copy).then_inc(S["xTe"], 1)

            def tile(t, first):
                key_blocks(act, t, first, n, pair, pair)
                for f in range(2):
                    window(t * 2 + f, f, P, 2 * P)
                tail(t, P)
            tiles(act, tile)

            softplus_part(z[0:TS, 0:256], S["cz"], 1, S["cln"])
            act.wait_ge(S["ctri"], 1)
            nc.scalar.activation(probs[0:TS, 0:256], z[0:TS, 0:256], ACT.Exp).then_inc(S["ca"], 1)
            with act.Fori(1, 5) as g:
                act.wait_ge(S["tk"], g * 2 - 1)
                act.wait_ge(S["cz"], g)
                nc.scalar.activation(cache_kT[:, 0:2, :, :].rearrange("p b m s -> p (b m s)"), z[:, 1024:2048],
                                     ACT.Copy).then_inc(S["ckT"], 1)
                softplus_part(z[:, 0:1024], S["cz"], g + 1, S["cln"])
                act.wait_ge(S["ctri"], g + 1)
                act.wait_ge(S["cpv"], g)
                nc.scalar.activation(probs[:], z[:, 0:1024], ACT.Exp).then_inc(S["ca"], 1)
            act.wait_ge(S["kws_turn"], 1)
            act.wait_ge(S["qs_in"], N_QS * 16)
            nc.scalar.activation(kws[:, :, 0:WIN], wide[:, 0:256].rearrange("p (n s) -> p n s", n=2),
                                 ACT.Copy).then_inc(S["kws_copied"], 1)
            for f in range(2):
                window(NT * 2 + f, f, TS, WIN + TS)
            tail(NT, TS)

        @block.vector
        def _(dve):
            dve.wait_ge(S["const"], 12 * 16)
            n = counter(dve)

            def softplus(n, diagonal):
                dve.wait_ge(S["ln"], n + 1)
                nc.vector.scalar_tensor_tensor(sp[:], z[:, bass.ds((n % 2) * 1024, 1024)], 0.0, soft[:],
                                               ALU.max, ALU.add)

            def diagonal(n, t, j):
                dve.wait_ge(S["tri"], n + 1)
                nc.vector.memset(later[:], 0.0)
                dve.wait_ge(S["ln"], n + 1)
                nc.vector.scalar_tensor_tensor(sp[:], z[:, bass.ds((n % 2) * 1024, 1024)], 0.0, soft[:],
                                               ALU.max, ALU.add)
                dve.drain()
                view = sp[:].rearrange("p (h q) -> p h q", h=NH)
                nc.vector.tensor_tensor(view, view, visible[:].unsqueeze(1).broadcast_to([P, NH, P]),
                                        ALU.mult).then_inc(S["sp"], 1)

            def earlier(n, t, j):
                dve.wait_ge(S["tri"], n + 1)
                nc.vector.tensor_tensor(later[:], later[:], sp[:], ALU.add)
                dve.drain()
                dve.wait_ge(S["ln"], n + 1)
                nc.vector.scalar_tensor_tensor(sp[:], z[:, bass.ds((n % 2) * 1024, 1024)], 0.0, soft[:],
                                               ALU.max, ALU.add).then_inc(S["sp"], 1)

            def window(u, f, rows, keys, bias):
                dve.wait_ge(S["zs"], u + 1)
                dve.wait_ge(S["tp"], u)
                scores = win_s[0:rows, :, 0:keys]
                nc.vector.tensor_tensor(scores, wide[0:rows, :].rearrange("p (h k) -> p h k", h=4)[:, :, 0:keys],
                                        bias, ALU.add)
                dve.drain()
                nc.vector.tensor_reduce(win[0:rows, 0, :], scores, AXX, ALU.max)
                dve.drain()
                nc.vector.tensor_tensor(win[0:rows, 1, :], win[0:rows, 0, :], sinks[0:rows, 4 * f:4 * f + 4], ALU.max)
                dve.drain()
                nc.vector.tensor_tensor(win[0:rows, 3, :], sinks[0:rows, 4 * f:4 * f + 4], win[0:rows, 1, :],
                                        ALU.subtract)
                nc.vector.tensor_scalar(win[0:rows, 2, :], win[0:rows, 1, :], -1.0, None, ALU.mult).then_inc(S["nm"], 1)
                dve.wait_ge(S["p"], u + 1)
                nc.vector.tensor_tensor(win[0:rows, 4, :], win[0:rows, 4, :], win[0:rows, 5, :], ALU.add)
                dve.drain()
                nc.vector.reciprocal(rden[0:rows, 4 * f:4 * f + 4], win[0:rows, 4, :])

            def tail(t, rows):
                hold(dve, S["pvw"], t * 2 + 2)
                hold(dve, S["pv"] if rows == P else S["cpv"], dve.snap(n) + 1 if rows == P else 5)
                dve.drain()
                nc.vector.tensor_tensor(
                    merged[0:rows, 512:1024].rearrange("p (h d) -> p h d", h=NH),
                    o_sw[0:rows, :].rearrange("p (h d) -> p h d", h=NH),
                    rden[0:rows, :].unsqueeze(2).broadcast_to([rows, NH, HD]), ALU.mult).then_inc(S["msw"], 1)
                dve.wait_ge(S["ssq"], t + 1)
                nc.vector.tensor_scalar(stat[0:rows, 1, :], stat[0:rows, 0, :], 1.0 / 512, EPS,
                                        ALU.mult, ALU.add).then_inc(S["mean2"], 1)
                dve.wait_ge(S["guess2"], t + 1)
                rsqrt_newton(nc, dve, stat[0:rows, 1, :], stat[0:rows, 3, :], stat[0:rows, 4, :], stat[0:rows, 5, :])
                dve.drain()
                nc.vector.tensor_scalar(merged[0:rows, 512:1024], merged[0:rows, 512:1024], stat[0:rows, 5, 1:2],
                                        None, ALU.mult).then_inc(S["mB"], 1)
                dve.wait_ge(S["tm"], t + 1)
                nc.vector.tensor_tensor(mergedT[:, :, 0:rows],
                                        wide[:].rearrange("p (k t) -> p k t", k=DK)[:, :, 0:rows],
                                        g_out[:].unsqueeze(2).broadcast_to([P, DK, rows]), ALU.mult).then_inc(S["mTe"], 1)
                dve.wait_ge(S["op"], t + 1)
                dve.wait_ge(S["x_in"], t * 16 + 16)
                dve.wait_ge(S["h_out"], t * 16)
                nc.vector.tensor_tensor(h[0:rows, :], wide[0:rows, :], x_res[0:rows, :], ALU.add).then_inc(S["h"], 1)
                dve.wait_ge(S["ssh"], t + 1)
                nc.vector.tensor_scalar(stat[0:rows, 1, 0:1], stat[0:rows, 0, 0:1], 1.0 / DM, EPS,
                                        ALU.mult, ALU.add).then_inc(S["meanh"], 1)
                dve.wait_ge(S["guessh"], t + 1)
                rsqrt_newton(nc, dve, stat[0:rows, 1, 0:1], stat[0:rows, 3, 0:1], stat[0:rows, 4, 0:1],
                             stat[0:rows, 5, 0:1])
                dve.drain()
                dve.wait_ge(S["xn_out"], t * 16)
                nc.vector.scalar_tensor_tensor(xn[0:rows, :], h[0:rows, :], stat[0:rows, 5, 0:1], g_ffn[0:rows, :],
                                               ALU.mult, ALU.mult).then_inc(S["xn"], 1)

            def tile(t, first):
                key_blocks(dve, t, first, n, diagonal, earlier)
                if not first:
                    dve.wait_ge(S["bias"], 16)
                for f in range(2):
                    window(t * 2 + f, f, P, 2 * P, alibi[:, 4 * f:4 * f + 4, :])
                tail(t, P)
            tiles(dve, tile)

            nc.vector.memset(later[:], 0.0)
            dve.drain()
            dve.wait_ge(S["cln"], 1)
            nc.vector.scalar_tensor_tensor(sp[0:TS, 0:256], z[0:TS, 0:256], 0.0, soft[0:TS, 0:256], ALU.max, ALU.add)
            dve.drain()
            view = sp[0:TS, 0:256].rearrange("p (h q) -> p h q", h=NH)
            own = visible[0:TS, 0:TS].unsqueeze(1).broadcast_to([TS, NH, TS])
            nc.vector.tensor_tensor(view, view, own, ALU.mult).then_inc(S["csp"], 1)
            dve.drain()
            nc.vector.tensor_copy(later[0:TS, 0:256], sp[0:TS, 0:256])
            dve.drain()
            with dve.Fori(1, 5) as g:
                dve.wait_ge(S["tk"], g * 2)
                dve.wait_ge(S["cz"], g)
                nc.vector.tensor_copy(cache_kT[:, 2:4, :, :].rearrange("p b m s -> p (b m s)"),
                                      wide[:]).then_inc(S["ckT"], 1)
                dve.wait_ge(S["ctri"], g)
                dve.wait_ge(S["cln"], g + 1)
                nc.vector.scalar_tensor_tensor(sp[:], z[:, 0:1024], 0.0, soft[:], ALU.max, ALU.add).then_inc(S["csp"], 1)
                hold(dve, S["ctri"], g + 1)
                for b in range(4):
                    dve.drain()
                    nc.vector.tensor_tensor(later[:, 0:256], later[:, 0:256], sp[:, b * 256:(b + 1) * 256], ALU.add)
                dve.drain()
            for f in range(2):
                window(NT * 2 + f, f, TS, WIN + TS, alibi_s[:, 4 * f:4 * f + 4, :])
            tail(NT, TS)

        @block.tensor
        def _(pe):
            pe.wait_ge(S["const"], 12 * 16)
            n = counter(pe)

            def scores(n):
                pe.wait_ge(S["k"], n * 16 + 16)
                for m in range(4):
                    last = nc.tensor.matmul(z[:, bass.ds((n % 2) * 1024 + m * 256, 256)], kT[:, m, :],
                                            q_pad[:, m, :, :].rearrange("p a q -> p (a q)"),
                                            start=(m % 2 == 0), stop=False, skip_group_check=True)
                last.then_inc(S["z"], 1)

            def pair(n, diagonal):
                scores(n + 1)
                pe.wait_ge(S["sp"], n + 1)
                for b in range(2):
                    out = z[:, bass.ds((n % 2) * 1024 + b * 512, 512)]
                    cols = slice(b * 512, (b + 1) * 512)
                    nc.tensor.matmul(out, neg_suffix[:], sp[:, cols], start=False, stop=False, skip_group_check=True)
                    if diagonal:
                        last = nc.tensor.matmul(out, ident[:], hidden[:], start=False, stop=True,
                                                skip_group_check=True)
                    else:
                        last = nc.tensor.matmul(out, neg_ones[:], later[:, cols], start=False, stop=True,
                                                skip_group_check=True)
                last.then_inc(S["tri"], 1)
                pe.wait_ge(S["a"], n + 1)
                pe.wait_ge(S["v"], n * 16 + 16)
                for hd in range(NH):
                    last = nc.tensor.matmul(o_sb[:, hd * HD:(hd + 1) * HD], probs[:, hd * P:(hd + 1) * P],
                                            v_blk[:, hd * HD:(hd + 1) * HD], start=(diagonal and hd == 0),
                                            stop=False, skip_group_check=True)
                last.then_inc(S["pv"], 1)

            def window(u, f, rows, blocks, queries, keys, values):
                for hh in range(4):
                    hd = 4 * f + hh
                    width = sum(blocks)
                    last = nc.tensor.matmul(wide[0:rows, hh * 256:hh * 256 + width], queries[:, hd // 2, hd % 2, :],
                                            keys[:, f, 0:width], start=(hh % 2 == 0), stop=True, skip_group_check=True)
                last.then_inc(S["zs"], 1)
                pe.wait_ge(S["p"], u + 1)
                for hh in range(4):
                    for b, size in enumerate(blocks):
                        i = 2 * hh + b
                        last = nc.tensor.transpose(wide[0:size, i * P:i * P + rows],
                                                   win_s[0:rows, hh, b * P:b * P + size], ident[0:rows, 0:rows])
                last.then_inc(S["tp"], 1)
                pe.wait_ge(S["pTe"], u + 1)
                for hh in range(4):
                    hd = 4 * f + hh
                    for b, size in enumerate(blocks):
                        last = nc.tensor.matmul(o_sw[0:rows, hd * HD:(hd + 1) * HD],
                                                win_pT[0:size, 2 * hh + b, 0:rows],
                                                values[0:size, b, f * HD:(f + 1) * HD],
                                                start=(hd == 0 and b == 0), stop=False, skip_group_check=True)
                last.then_inc(S["pvw"], 1)

            def tail(t, rows):
                pe.wait_ge(S["mA"], t + 1)
                pe.wait_ge(S["mB"], t + 1)
                for k in range(DK):
                    last = nc.tensor.transpose(wide[:, k * P:k * P + rows], merged[0:rows, k * P:(k + 1) * P],
                                               ident[0:rows, 0:rows])
                last.then_inc(S["tm"], 1)
                pe.wait_ge(S["mTe"], t + 1)
                for k in range(DK):
                    for b in range(2):
                        last = nc.tensor.matmul(wide[0:rows, b * 512:(b + 1) * 512], mergedT[:, k, 0:rows],
                                                w_out[:, k, b * 512:(b + 1) * 512], start=(k == 0),
                                                stop=(k == DK - 1), skip_group_check=True)
                last.then_inc(S["op"], 1)
                pe.wait_ge(S["xn"], t + 1)
                for k in range(DK):
                    last = nc.tensor.transpose(wide[:, k * P:k * P + rows], xn[0:rows, k * P:(k + 1) * P],
                                               ident[0:rows, 0:rows])
                last.then_inc(S["tx"], 1)

            for name in ("z", "tri", "pv"):
                pe.sem_inc(S[name], 1)
            scores(0)

            def tile(t, first):
                key_blocks(pe, t, first, n, lambda n, t, j: pair(n, True), lambda n, t, j: pair(n, False))
                pe.wait_ge(S["sw_in"], 8 * 16 if first else t * 96 + 128)
                pe.wait_ge(S["xTe"], t)
                for f in range(2):
                    window(t * 2 + f, f, P, (P, P), qw_pad, kw, vw)
                tail(t, P)
            tiles(pe, tile)

            pe.wait_ge(S["qs_in"], N_QS * 16)
            for m in range(4):
                last = nc.tensor.matmul(z[0:TS, m * 64:m * 64 + 64], ksT[:, m, :],
                                        qs_pad[:, m, :, :].rearrange("p a q -> p (a q)"),
                                        start=(m == 0), stop=False, skip_group_check=True)
            last.then_inc(S["cz"], 1)
            pe.wait_ge(S["csp"], 1)
            nc.tensor.matmul(z[0:TS, 0:256], neg_suffix[0:TS, 0:TS], sp[0:TS, 0:256], start=False, stop=False,
                             skip_group_check=True)
            for b in range(2):
                last = nc.tensor.matmul(z[0:TS, b * P:(b + 1) * P], ident[0:TS, 0:TS],
                                        hidden[0:TS, :].rearrange("p (r q) -> p r q", r=4)[:, :, 0:TS],
                                        start=False, stop=True, skip_group_check=True)
            last.then_inc(S["ctri"], 1)
            pe.wait_ge(S["ca"], 1)
            for hd in range(NH):
                last = nc.tensor.matmul(o_sb[0:TS, hd * HD:(hd + 1) * HD], probs[0:TS, hd * TS:(hd + 1) * TS],
                                        vs_blk[:, hd * HD:(hd + 1) * HD], start=(hd == 0), stop=False,
                                        skip_group_check=True)
            last.then_inc(S["cpv"], 1)
            with pe.Fori(1, 5) as g:
                pe.wait_ge(S["ck"], g * 16)
                for b in range(4):
                    dst = z[:, 1024 + b * 512:1536 + b * 512] if b < 2 else wide[:, (b - 2) * 512:(b - 1) * 512]
                    for m in range(4):
                        last = nc.tensor.transpose(dst[:, m * P:(m + 1) * P], cache_k[:, b, m * P:(m + 1) * P], ident[:])
                    if b % 2:
                        last.then_inc(S["tk"], 1)
                pe.wait_ge(S["ckT"], g * 2)
                for b in range(4):
                    for m in range(4):
                        last = nc.tensor.matmul(z[:, b * 256 + m * 64:b * 256 + m * 64 + 64], cache_kT[:, b, m, :],
                                                qs_pad[:, m, :, :].rearrange("p a q -> p (a q)"),
                                                start=(m == 0 and b % 2 == 0), stop=False, skip_group_check=True)
                last.then_inc(S["cz"], 1)
                pe.wait_ge(S["csp"], g + 1)
                for b in range(4):
                    out = z[:, b * 256:(b + 1) * 256]
                    nc.tensor.matmul(out, neg_suffix[:], sp[:, b * 256:(b + 1) * 256], start=False, stop=False,
                                     skip_group_check=True)
                    for b2 in range(b + 1, 4):
                        nc.tensor.matmul(out, neg_ones[:], sp[:, b2 * 256:(b2 + 1) * 256], start=False, stop=False,
                                         skip_group_check=True)
                    last = nc.tensor.matmul(out, neg_ones[:], later[:, 0:256], start=False, stop=True,
                                            skip_group_check=True)
                last.then_inc(S["ctri"], 1)
                pe.wait_ge(S["ca"], g + 1)
                pe.wait_ge(S["cv"], g * 16)
                for b in range(4):
                    for hd in range(NH):
                        last = nc.tensor.matmul(o_sb[0:TS, hd * HD:(hd + 1) * HD],
                                                probs[:, b * 256 + hd * TS:b * 256 + (hd + 1) * TS],
                                                cache_v[:, b, hd * HD:(hd + 1) * HD], start=False, stop=False,
                                                skip_group_check=True)
                last.then_inc(S["cpv"], 1)
            for kv in range(2):
                last = nc.tensor.transpose(wide[:, kv * P:(kv + 1) * P],
                                           kws_in[:, kv, :, :].rearrange("p a d -> p (a d)"), ident[:])
            last.then_inc(S["kws_turn"], 1)
            pe.wait_ge(S["kws_copied"], 1)
            for f in range(2):
                window(NT * 2 + f, f, TS, (WIN, TS), qws_pad, kws, vws)
            tail(NT, TS)


def expert_phase(nc, io):
    with ExitStack() as ctx:
        def sb(name, shape, dt=F32):
            return ctx.enter_context(nc.sbuf_tensor("ex_" + name, shape, dt))
        ps = lambda name, shape: ctx.enter_context(nc.psum_tensor("ex_" + name, shape, F32))
        sem = lambda name: ctx.enter_context(nc.semaphore("e_" + name))

        ident = sb("ident", [P, P])
        fold = sb("fold", [P, TS])
        iota = sb("iota", [P, NCAND])
        g_final = sb("g_final", [P, DM])
        w_q = sb("w_q", [P, DK, PH * 2 * QH])
        keys = sb("keys", [P, 2, QH])
        keysT = sb("keysT", [P, 2, NKEY])
        xT = sb("xT", [P, DK, P])
        q = sb("q", [P, 2 * QH])
        qT = sb("qT", [P, 2, P])
        cut = sb("cut", [P, 2, NKEY])
        val = sb("val", [P, 2, TOPK])
        ind = sb("ind", [P, 2, TOPK], U32)
        indf = sb("indf", [P, 2, TOPK])
        row = sb("row", [P, TOPK])
        cand = sb("cand", [P, 2, NCAND])
        cand_cut = sb("cand_cut", [P, NCAND])
        best = sb("best", [P, TOPK])
        pos = sb("pos", [P, TOPK], U32)
        posf = sb("posf", [P, TOPK])
        pick = sb("pick", [P, TOPK, NCAND])
        idxf = sb("idxf", [P, TOPK])
        gate = sb("gate", [P, TOPK])
        soft = sb("soft", [P, 3])
        idx_all = sb("idx_all", [P, (NT + 1) * SLOTS], U32)
        gate_all = sb("gate_all", [P, (NT + 1) * SLOTS])
        idx = sb("idx", [P, 2, TOPK], U32)
        idx_sample = sb("idx_sample", [P, 2, TOPK], U32)
        u_row = sb("u_row", [P, RING, DM])
        v_row = sb("v_row", [P, RING, DM])
        hid = sb("hid", [P, 2, TOPK])
        act_hid = sb("act_hid", [P, 2, TOPK])
        weight = sb("weight", [P, 2, TOPK])
        diag = sb("diag", [P, 2, TOPK, P])
        x_tok = sb("x_tok", [P, DM])
        h = sb("h", [P, DM])
        y = sb("y", [P, DM])
        y_out = sb("y_out", [P, DM])
        stat = sb("stat", [P, 6])

        y_acc = ps("y_acc", [P, DM])
        x_ps = ps("x_ps", [P, DM])
        q_ps = ps("q_ps", [P, 512])
        qT_ps = ps("qT_ps", [P, 512])
        s_ps = ps("s_ps", [P, 512])

        names = """idx shared const keys_turn keys_copied xT q qe qt qTe scores best gate_exp routed
                   dot gelu weight diag vmm x_in x_ps h_in y_zero y squares mean guess y_out y_stored""".split()
        S = {n: sem(n) for n in names}
        S_U = [sem(f"u_row{i}") for i in range(RING)]
        S_V = [sem(f"v_row{i}") for i in range(RING)]
        DOT0 = RING
        VMM0 = RING + TOPK
        block = ctx.enter_context(nc.Block())

        def tiles(engine, tile):
            with engine.Fori(0, NT) as t:
                tile(t, P)
            tile(NT, TS)

        def units(engine, t, rows, unit):
            if rows == P:
                with engine.Fori(0, PH // 2) as pair:
                    for e in range(2):
                        unit(t * PH + pair * 2 + e, e, pair * 2 + e)
            else:
                for e in range(2):
                    unit(t * PH + e, e, None)

        def share(table, e, c):
            per_head = table[c * TS:(c + 1) * TS, NT * SLOTS:].rearrange("p (h k) -> p h k", h=PH)
            return per_head[:, 4 * e:4 * e + 4, c * PART:(c + 1) * PART]

        def shared(table, e, c):
            return table[c * TS:(c + 1) * TS, e, :].rearrange("p (h k) -> p h k", h=4)

        @block.sync
        def _(sync):
            for dst, src in ((ident[:], io["ident"]), (fold[:], io["fold"]), (iota[:], io["rank_iota"]),
                             (g_final[:], io["norm_final"].partition_broadcast(P)),
                             (keys[:, 0, :], io["peer_keys_1"]), (keys[:, 1, :], io["peer_keys_2"]),
                             (w_q[:], io["w_peer_q"].rearrange("(k p) n -> p k n", p=P))):
                sync.dma_start(dst, src).then_inc(S["const"], 16)

            def load_xT(t):
                hold(sync, S["q"], t * PH)
                sync.dma_start(xT[:].rearrange("p k t -> p (k t)"), io["xn2T"][t, :, :]).then_inc(S["xT"], 16)

            def load_x(t, rows, tokens):
                hold(sync, S["x_ps"], t)
                for first in range(0, P, rows):
                    sync.dma_start(x_tok[first:first + rows, :], io["xn2"][tokens, :]).then_inc(S["x_in"], 16)

            def load_h(t, rows, tokens):
                if not isinstance(t, int) or t > 0:
                    hold(sync, S["y_stored"], t * 16)
                sync.dma_start(h[0:rows, :], io["h"][tokens, :]).then_inc(S["h_in"], 16)

            def store(t, rows, dst):
                hold(sync, S["y_out"], t + 1)
                sync.dma_start(dst, y_out[0:rows, :]).then_inc(S["y_stored"], 16)

            prompt = io["y_prompt"].rearrange("a t d -> (a t) d")
            load_xT(0)
            load_x(0, P, slice(0, P))
            load_xT(1)
            load_h(0, P, slice(0, P))
            with sync.Fori(1, NT) as t:
                load_x(t, P, bass.ds(t * P, P))
                load_xT(t + 1)
                store(t - 1, P, prompt[bass.ds(t * P - P, P), :])
                load_h(t, P, bass.ds(t * P, P))
            load_x(NT, TS, slice(SEQ, TOK))
            store(NT - 1, P, prompt[SEQ - P:SEQ, :])
            load_h(NT, TS, slice(SEQ, TOK))
            store(NT, TS, io["y_sample"].rearrange("a t d -> (a t) d"))
            sync.wait_ge(S["y_stored"], (NT + 1) * 16)

        @block.gpsimd
        def _(pool):
            def tile(t, rows):
                def unit(u, e, head):
                    if rows == P:
                        hold(pool, S["routed"], u + 2)
                        nc.gpsimd.tensor_copy(idx[:, e, :], idx_all[:, bass.ds(u * TOPK, TOPK)]).then_inc(S["idx"], 1)
                        hold(pool, S["idx"], u + 1)
                    else:
                        hold(pool, S["shared"], 1)
                    rows_of = idx if rows == P else idx_sample
                    for table, ring, landed, free, credits in (("peer_u", u_row, S_U, "dot", DOT0),
                                                               ("peer_v", v_row, S_V, "vmm", VMM0)):
                        for k in range(TOPK):
                            hold(pool, S[free], u * TOPK + (k + 1 + credits - RING))
                            pool.indirect_dma_start(
                                ring[:, k % RING, :], None, io[table],
                                bass.IndirectOffsetOnAxis(ap=rows_of[:, e, k:k + 1], axis=0),
                            ).then_inc(landed[k % RING], 16)
                units(pool, t, rows, unit)
            tiles(pool, tile)

        @block.scalar
        def _(act):
            def route_queries(m):
                act.wait_ge(S["q"], m + 1)
                nc.scalar.activation(q[:], q_ps[:, 0:2 * QH], ACT.Copy).then_inc(S["qe"], 1)
                act.wait_ge(S["qt"], m + 1)
                nc.scalar.activation(qT[:].rearrange("p f t -> p (f t)"), qT_ps[:, 0:2 * P],
                                     ACT.Copy).then_inc(S["qTe"], 1)

            def route_gates(m):
                act.wait_ge(S["best"], m + 1)
                nc.scalar.activation(gate[:], best[:], ACT.Exp, bias=soft[:, 0:1],
                                     accum_out=soft[:, 1:2]).then_inc(S["gate_exp"], 1)

            act.sem_inc(S["qe"], 1)
            act.wait_ge(S["keys_turn"], 1)
            nc.scalar.activation(keysT[:].rearrange("p f n -> p (f n)"), qT_ps[:, 0:2 * NKEY],
                                 ACT.Copy).then_inc(S["keys_copied"], 1)
            with act.Fori(0, PH) as head:
                route_queries(head)
                route_gates(head)

            def tile(t, rows):
                act.wait_ge(S["x_in"], t * 16 + (16 if rows == P else 16 * COPIES))
                act.wait_ge(S["dot"], t * SLOTS + DOT0)
                nc.scalar.activation(x_ps[:], x_tok[:], ACT.Copy).then_inc(S["x_ps"], 1)

                def unit(u, e, head):
                    if rows == P:
                        route_queries(u + PH)
                    act.wait_ge(S["dot"], u * TOPK + (TOPK + DOT0))
                    nc.scalar.activation(act_hid[:, e, :], hid[:, e, :], ACT.Gelu).then_inc(S["gelu"], 1)
                    act.wait_ge(S["vmm"], u * TOPK + (VMM0 - TOPK))
                    act.wait_ge(S["weight"], u + 1)
                    for k in range(TOPK):
                        made = nc.scalar.activation(diag[:, e, k, 0:rows], (ident if rows == P else fold)[:], ACT.Copy,
                                                    scale=weight[:, e, k:k + 1])
                        if k % 4 == 3:
                            made.then_inc(S["diag"], 1)
                    if rows == P:
                        route_gates(u + PH)
                units(act, t, rows, unit)
                act.wait_ge(S["y"], t + 1)
                nc.scalar.activation(y_out[0:rows, :], y[0:rows, :], ACT.Square,
                                     accum_out=stat[0:rows, 0:1]).then_inc(S["squares"], 1)
                act.wait_ge(S["mean"], t + 1)
                rsqrt_guess(nc, act, stat[0:rows, 1:2], stat[0:rows, 2:3], stat[0:rows, 3:4]).then_inc(S["guess"], 1)
            tiles(act, tile)

        @block.vector
        def _(dve):
            dve.sem_inc(S["dot"], DOT0)
            dve.sem_inc(S["routed"], 1)
            dve.wait_ge(S["const"], 7 * 16)

            def top16(values, rest, out, where):
                for v, o in zip(values, out):
                    nc.vector.max(o[:, 0:8], v)
                dve.drain()
                for v, r, o, w in zip(values, rest, out, where):
                    nc.vector.max_index(w[:, 0:8], o[:, 0:8], v)
                    nc.vector.match_replace(r, o[:, 0:8], v, LOWEST)
                dve.drain()
                for r, o in zip(rest, out):
                    nc.vector.max(o[:, 8:16], r)
                dve.drain()
                for r, o, w in zip(rest, out, where):
                    nc.vector.max_index(w[:, 8:16], o[:, 8:16], r)
                dve.drain()

            def route(m):
                hold(dve, S["scores"], m + 1)
                top16([s_ps[:, f * NKEY:(f + 1) * NKEY] for f in range(2)], [cut[:, f, :] for f in range(2)],
                      [val[:, f, :] for f in range(2)], [ind[:, f, :] for f in range(2)])
                nc.vector.tensor_copy(indf[:], ind[:])
                dve.drain()
                nc.vector.tensor_scalar(row[:], indf[:, 0, :], float(NKEY), None, ALU.mult)
                dve.drain()
                for o, a, b in ((cand[:, 0, :], val[:, 0, :], val[:, 1, :]), (cand[:, 1, :], row, indf[:, 1, :])):
                    at = 0
                    for r in range(5):
                        n = PAIR_ROWS[r][1]
                        nc.vector.tensor_scalar(o[:, at:at + n], b[:, 0:n], a[:, r:r + 1], None, ALU.add)
                        at += n
                    nc.vector.tensor_tensor(o[:, at:at + 6].rearrange("p (r n) -> p r n", r=3),
                                            a[:, 5:8].unsqueeze(2).broadcast_to([P, 3, 2]),
                                            b[:, 0:2].unsqueeze(1).broadcast_to([P, 3, 2]), ALU.add)
                    nc.vector.tensor_scalar(o[:, at + 6:at + 14], a[:, 8:16], b[:, 0:1], None, ALU.add)
                    assert at + 14 == NCAND
                dve.drain()
                top16([cand[:, 0, :]], [cand_cut[:]], [best], [pos])
                nc.vector.tensor_scalar(soft[:, 0:1], best[:, 0:1], -1.0, None, ALU.mult).then_inc(S["best"], 1)
                nc.vector.tensor_copy(posf[:], pos[:])
                dve.drain()
                full = [P, TOPK, NCAND]
                nc.vector.tensor_tensor(pick[:], iota[:].unsqueeze(1).broadcast_to(full),
                                        posf[:].unsqueeze(2).broadcast_to(full), ALU.is_equal)
                dve.drain()
                nc.vector.tensor_tensor(pick[:], pick[:], cand[:, 1, :].unsqueeze(1).broadcast_to(full), ALU.mult)
                dve.drain()
                nc.vector.tensor_reduce(idxf[:], pick[:], AXX, ALU.add)
                dve.drain()
                nc.vector.tensor_copy(idx_all[:, bass.ds(m * TOPK, TOPK)], idxf[:])
                dve.wait_ge(S["gate_exp"], m + 1)
                nc.vector.reciprocal(soft[:, 2:3], soft[:, 1:2])
                dve.drain()
                nc.vector.tensor_scalar(gate_all[:, bass.ds(m * TOPK, TOPK)], gate[:], soft[:, 2:3], None,
                                        ALU.mult).then_inc(S["routed"], 1)

            with dve.Fori(0, PH) as head:
                route(head)

            def tile(t, rows):
                if rows < P:
                    for e in range(2):
                        for c in range(COPIES):
                            nc.vector.tensor_copy(shared(idx_sample, e, c), share(idx_all, e, c))
                    dve.drain()
                    dve.sem_inc(S["shared"], 1)
                dve.drain()
                nc.vector.memset(y_acc[0:rows, :], 0.0).then_inc(S["y_zero"], 1)
                hold(dve, S["x_ps"], t + 1)

                def unit(u, e, head):
                    for k in range(TOPK):
                        dve.wait_ge(S_U[k % RING], u * 32 + (k // RING + 1) * 16)
                        slot = u_row[:, k % RING, :]
                        nc.vector.tensor_tensor_reduce(slot, slot, x_ps[:], 1.0, 0.0, ALU.mult, ALU.add,
                                                       hid[:, e, k:k + 1]).then_inc(S["dot"], 1)
                    hold(dve, S["gelu"], u + 1)
                    if rows == P:
                        nc.vector.tensor_tensor(weight[:, e, :], act_hid[:, e, :],
                                                gate_all[:, bass.ds(u * TOPK, TOPK)], ALU.mult).then_inc(S["weight"], 1)
                    else:
                        for c in range(COPIES):
                            nc.vector.tensor_tensor(shared(weight, e, c), shared(act_hid, e, c),
                                                    share(gate_all, e, c), ALU.mult)
                        dve.drain()
                        dve.sem_inc(S["weight"], 1)
                    if rows == P:
                        route(u + PH)
                units(dve, t, rows, unit)
                dve.wait_ge(S["h_in"], t * 16 + 16)
                dve.wait_ge(S["vmm"], t * SLOTS + ((SLOTS if rows == P else 2 * TOPK) + VMM0))
                nc.vector.tensor_tensor(y[0:rows, :], y_acc[0:rows, :], h[0:rows, :], ALU.add)
                dve.drain()
                dve.sem_inc(S["y"], 1)
                dve.wait_ge(S["squares"], t + 1)
                nc.vector.tensor_scalar(stat[0:rows, 1:2], stat[0:rows, 0:1], 1.0 / DM, EPS,
                                        ALU.mult, ALU.add).then_inc(S["mean"], 1)
                dve.wait_ge(S["guess"], t + 1)
                rsqrt_newton(nc, dve, stat[0:rows, 1:2], stat[0:rows, 3:4], stat[0:rows, 4:5], stat[0:rows, 5:6])
                dve.drain()
                nc.vector.scalar_tensor_tensor(y_out[0:rows, :], y[0:rows, :], stat[0:rows, 5:6], g_final[0:rows, :],
                                               ALU.mult, ALU.mult).then_inc(S["y_out"], 1)
            tiles(dve, tile)

        @block.tensor
        def _(pe):
            pe.sem_inc(S["vmm"], VMM0)
            pe.wait_ge(S["const"], 7 * 16)
            for f in range(2):
                last = nc.tensor.transpose(qT_ps[:, f * NKEY:(f + 1) * NKEY], keys[:, f, :], ident[:])
            last.then_inc(S["keys_turn"], 1)
            pe.wait_ge(S["keys_copied"], 1)

            def route(m, t, head):
                pe.wait_ge(S["xT"], t * 16 + 16)
                pe.wait_ge(S["qe"], m + 1)
                for k in range(DK):
                    last = nc.tensor.matmul(q_ps[:, 0:2 * QH], xT[:, k, :], w_q[:, k, bass.ds(head * 2 * QH, 2 * QH)],
                                            start=(k == 0), stop=(k == DK - 1))
                last.then_inc(S["q"], 1)
                pe.wait_ge(S["qe"], m + 2)
                for f in range(2):
                    last = nc.tensor.transpose(qT_ps[:, f * P:(f + 1) * P], q[:, f * QH:(f + 1) * QH], ident[:])
                last.then_inc(S["qt"], 1)
                pe.wait_ge(S["qTe"], m + 1)
                pe.wait_ge(S["routed"], m + 1)
                for f in range(2):
                    last = nc.tensor.matmul(s_ps[:, f * NKEY:(f + 1) * NKEY], qT[:, f, :], keysT[:, f, :],
                                            start=True, stop=True)
                last.then_inc(S["scores"], 1)

            with pe.Fori(0, PH) as head:
                route(head, 0, head)

            def tile(t, rows):
                hold(pe, S["y_zero"], t + 1)

                def unit(u, e, head):
                    if rows == P:
                        route(u + PH, t + 1, head)
                    for k in range(TOPK):
                        if k % 4 == 0:
                            pe.wait_ge(S["diag"], u * 4 + (k // 4 + 1))
                        pe.wait_ge(S_V[k % RING], u * 32 + (k // RING + 1) * 16)
                        for b in range(2):
                            last = nc.tensor.matmul(y_acc[0:rows, b * 512:(b + 1) * 512], diag[:, e, k, 0:rows],
                                                    v_row[:, k % RING, b * 512:(b + 1) * 512],
                                                    start=False, stop=True, skip_group_check=True)
                        last.then_inc(S["vmm"], 1)
                units(pe, t, rows, unit)
            tiles(pe, tile)


PHASES = [projection_phase, attention_phase, expert_phase]
OUTPUTS = {
    "y_prompt": (1, SEQ, DM), "y_sample": (1, TS, DM),
    "sb_k_prompt": (1, 1, SEQ, NH, HD), "sb_v_prompt": (1, 1, SEQ, NH, HD),
    "swa_k_prompt": (1, 1, WIN, 2, HD), "swa_v_prompt": (1, 1, WIN, 2, HD),
    "sb_k_sample": (1, 1, TS, NH, HD), "sb_v_sample": (1, 1, TS, NH, HD),
    "swa_k_sample": (1, 1, WIN, 2, HD), "swa_v_sample": (1, 1, WIN, 2, HD),
}
SCRATCH = {
    "projT": (C_END, P, TOK),
    "nat": (TOK, NATW),
    "h": (TOK, DM),
    "xn2": (TOK, DM),
    "xn2T": (NT + 1, P, DK * P),
}
INPUT_SHAPES = {
    "x_prompt": (SEQ, DM), "x_sample": (TS, DM), "cache_sb_k": (PAST, SBW), "cache_sb_v": (PAST, SBW),
    "cache_swa_k": (WIN, KVW), "cache_swa_v": (WIN, KVW), "norm_mix": (1, DM), "w_in": (DM, INW),
    "swa_sinks": (1, NH), "norm_sb_out": (1, SBW), "norm_swa_out": (1, SBW), "w_out": (2 * SBW, DM),
    "norm_ffn": (1, DM), "w_peer_q": (DM, PH * 2 * QH), "peer_keys_1": (NKEY, QH), "peer_keys_2": (NKEY, QH),
    "peer_u": (NKEY * NKEY, DM), "peer_v": (NKEY * NKEY, DM), "norm_final": (1, DM),
}


def lay_out(inputs):
    arrays = {n: np.ascontiguousarray(inputs[n]).reshape(shape) for n, shape in INPUT_SHAPES.items()}
    arrays.update(constants())
    return arrays


def kernel(**inputs):
    import concourse.bacc as _bacc
    from concourse.bass_utils import run_bass_kernel_spmd as _run

    nc = _bacc.Bacc("TRN2", target_bir_lowering=False, num_devices=1)
    arrays = lay_out(inputs)
    io = {n: nc.dram_tensor(n, a.shape, F32, kind="ExternalInput").ap() for n, a in arrays.items()}
    for n, shape in OUTPUTS.items():
        io[n] = nc.dram_tensor(f"out_{n}", shape, F32, kind="ExternalOutput").ap()
    for n, shape in SCRATCH.items():
        io[n] = nc.dram_tensor(f"scratch_{n}", shape, F32, kind="Internal").ap()
    for phase in PHASES:
        phase(nc, io)
    r = _run(nc, [arrays], core_ids=[0])
    return tuple(r.results[0][f"out_{n}"] for n in OUTPUTS)
```

```python
from contextlib import ExitStack

import numpy as np

import concourse.bass as bass
from concourse import mybir

ALU = mybir.AluOpType
ACT = mybir.ActivationFunctionType
AXX = mybir.AxisListType.X
F32 = mybir.dt.float32
U32 = mybir.dt.uint32

P = 128
DM = 1024
DK = DM // P
SEQ = 1024
NT = SEQ // P
TS = 32
TOK = SEQ + TS
PAST = 2048
HD = 64
NH = 8
SBW = NH * HD
WIN = 128
CHUNK = 64
KVW = 2 * HD
INW = 3 * SBW + SBW + 2 * KVW
C_QSB, C_KV, C_QSW, C_KVSW, C_END = 0, 4, 12, 16, 18
NATW = 2 * SBW + 2 * KVW
PH = 8
TOPK = 16
NKEY = 128
QH = 128
EPS = 1e-6
SCALE = HD ** -0.5
MASKED = -1e30
LOWEST = -3.0e38
PAIR_ROWS = [(a, TOPK // (a + 1)) for a in range(TOPK)]
NCAND = sum(n for _, n in PAIR_ROWS)
RING = 8
SLOTS = PH * TOPK
COPIES = P // TS
PART = TOPK // COPIES


def constants():
    s = np.arange(P)
    suffix = (s[:, None] >= s[None, :]).astype(np.float32)
    before = (s[:, None] < s[None, :]).astype(np.float32)
    c = {
        "ident": np.eye(P, dtype=np.float32),
        "neg_suffix": -suffix,
        "neg_ones": -np.ones((P, P), np.float32),
        "visible": before,
        "hidden": np.tile((1 - before) * np.float32(MASKED), (1, 4)).astype(np.float32),
        "rank_iota": np.tile(np.arange(NCAND, dtype=np.float32), (P, 1)),
    }
    slopes = (2.0 ** (-8.0 * np.arange(1, NH + 1, dtype=np.float32) / NH)).astype(np.float32)
    q, k = np.arange(P), np.arange(2 * P) - P
    dist = np.abs(q[:, None] - k[None, :]).astype(np.float32)
    lo = (q // CHUNK) * CHUNK - WIN
    seen = (k[None, :] >= lo[:, None]) & (k[None, :] < lo[:, None] + WIN + CHUNK)
    bias = np.where(seen[:, None, :], -slopes[None, :, None] * dist[:, None, :], MASKED)
    first = np.where((k >= 0)[None, None, :], bias, MASKED)
    c["alibi"] = np.stack([first, bias]).astype(np.float32).reshape(2, P, NH * 2 * P)
    qs, ks = np.arange(TS), np.arange(WIN + TS) - WIN
    dist = np.abs(qs[:, None] - ks[None, :]).astype(np.float32)
    c["fold"] = np.tile(np.eye(TS, dtype=np.float32), (P // TS, 1))
    c["alibi_sample"] = (-slopes[None, :, None] * dist[:, None, :]).astype(np.float32).reshape(TS, -1)
    return c


def rsqrt_guess(nc, act, mean, work, out):
    nc.scalar.activation(work, mean, ACT.Ln)
    act.drain()
    return nc.scalar.activation(out, work, ACT.Exp, scale=-0.5)


def rsqrt_newton(nc, dve, mean, guess, work, out):
    nc.vector.tensor_tensor(work, guess, guess, ALU.mult)
    dve.drain()
    nc.vector.tensor_tensor(work, work, mean, ALU.mult)
    dve.drain()
    nc.vector.tensor_scalar(work, work, -0.5, 1.5, ALU.mult, ALU.add)
    dve.drain()
    return nc.vector.tensor_tensor(out, work, guess, ALU.mult)


def hold(engine, sem, value):
    engine.wait_ge(sem, value)
    engine.nop(nofuse=True)


def tile_index(nc, j):
    if isinstance(j, int):
        return j
    return nc.s_assert_within(j, 0, NT - 1, skip_runtime_bounds_check_because="back runs below t")


def projection_phase(nc, io):
    with ExitStack() as ctx:
        sb = lambda name, shape: ctx.enter_context(nc.sbuf_tensor(name, shape, F32))
        ps = lambda name, shape: ctx.enter_context(nc.psum_tensor(name, shape, F32))
        sem = lambda name: ctx.enter_context(nc.semaphore(name))

        ident = sb("p1_ident", [P, P])
        g_mix = sb("g_mix", [P, DK])
        x_in = sb("x_in", [P, 4, DM])
        squares = sb("squares", [P, 2, DM])
        stat = sb("p1_stat", [P, 4, 6])
        xnT = sb("xnT", [P, DK, TOK])
        w = sb("w_cols", [P, 2, DK, P])
        stage = sb("stage", [P, 2, TOK])
        nat = sb("nat", [P, 2, NT + 1, P])
        acc = [ps(f"proj{s}", [P, 3 * 512]) for s in range(2)]
        turn = ps("turn", [P, 2 * 512])

        s_const = sem("p1_const")
        s_x = [sem(f"x_loaded{s}") for s in range(4)]
        s_sq = sem("squares_summed")
        s_mean = sem("mean_ready")
        s_guess = sem("guess_ready")
        s_xs = sem("x_scaled")
        s_xT = sem("x_turned")
        s_xnT = sem("xnT_free")
        s_w = [sem(f"w_loaded{s}") for s in range(2)]
        s_mm = sem("projected")
        s_evA = sem("stage_by_act")
        s_evD = sem("stage_by_dve")
        s_st = [sem(f"stage_stored{s}") for s in range(2)]
        s_tr = sem("natural_turned")
        s_nat = sem("natural_ready")
        s_ns = [sem(f"natural_stored{s}") for s in range(2)]
        block = ctx.enter_context(nc.Block())

        def tiles(engine, step, later=None):
            with engine.Fori(0, NT // 4) as four:
                for s in range(4):
                    step(four * 4 + s, s, four, P)
                    if later and s > 0:
                        later(four * 4 + (s - 1), s - 1, P)
                if later:
                    later(four * 4 + 3, 3, P)
            step(NT, 0, NT // 4, TS)
            if later:
                later(NT, 0, TS)

        def columns(engine, steps):
            for lo, hi, kv0 in ((C_QSB, C_KV, None), (C_KV, C_QSW, 0), (C_QSW, C_KVSW, None),
                                (C_KVSW, C_END, C_QSW - C_KV)):
                def run(pair):
                    for step in steps:
                        for s in range(2):
                            kv = None if kv0 is None else pair * 2 + (s + kv0 - lo)
                            step(pair * 2 + s, s, pair, kv, lo)
                run(lo // 2)
                if hi - lo > 2:
                    with engine.Fori(lo // 2 + 1, hi // 2) as pair:
                        run(pair)

        @block.sync
        def _(sp):
            sp.dma_start(ident[:], io["ident"]).then_inc(s_const, 16)
            sp.dma_start(g_mix[:], io["norm_mix"].rearrange("o (k p) -> p (o k)", p=P),
                         allow_slow_non_contiguous=True).then_inc(s_const, 16)

            for t in range(NT + 1):
                if t >= 4:
                    sp.wait_ge(s_xT, t - 3)
                rows, src = (P, io["x_prompt"][t * P:(t + 1) * P, :]) if t < NT else (TS, io["x_sample"])
                sp.dma_start(x_in[0:rows, t % 4, :], src).then_inc(s_x[t % 4], 16)

            def load_w(c, s):
                src = io["w_in"].rearrange("(k p) n -> p k n", p=P)[:, :, bass.ds(c * P, P)]
                sp.dma_start(w[:, s, :, :], src).then_inc(s_w[s], 16)
            load_w(0, 0)
            load_w(1, 1)
            with sp.Fori(0, C_END // 2 - 1) as pair:
                for s in range(2):
                    sp.wait_ge(s_mm, pair * 2 + (s + 1))
                    load_w(pair * 2 + (s + 2), s)

        @block.scalar
        def _(act):
            act.preload_act_table_set("natural_log_exp_and_others")

            def square(t, s, turn, rows):
                act.wait_ge(s_x[s], (turn + 1) * 16)
                nc.scalar.activation(squares[0:rows, s % 2, :], x_in[0:rows, s, :], ACT.Square,
                                     accum_out=stat[0:rows, s, 0:1]).then_inc(s_sq, 1)
                act.wait_ge(s_mean, t + 1)
                rsqrt_guess(nc, act, stat[0:rows, s, 1:2], stat[0:rows, s, 2:3],
                            stat[0:rows, s, 3:4]).then_inc(s_guess, 1)
            tiles(act, square)

            act.sem_inc(s_evA, 2)

            def evacuate(c, s, pair, kv, lo):
                act.wait_ge(s_mm, c + 1)
                act.wait_ge(s_st[s], pair * 16)
                act.wait_ge(s_tr, {C_QSB: 2, C_QSW: 10, C_KVSW: 10}[lo] if kv is None or lo == C_KVSW else kv + 1)
                scale = SCALE if kv is None else 1.0
                nc.scalar.activation(stage[:, s, 0:512], acc[s][:, 0:512], ACT.Copy, scale=scale)
                nc.scalar.activation(stage[:, s, SEQ:TOK], acc[s][:, 1024:1024 + TS], ACT.Copy,
                                     scale=scale).then_inc(s_evA, 1)
            columns(act, [evacuate])

        @block.vector
        def _(dve):
            dve.sem_inc(s_xnT, 2)
            dve.wait_ge(s_const, 32)

            def normalise(t, s, turn, rows):
                dve.wait_ge(s_sq, t + 1)
                nc.vector.tensor_scalar(stat[0:rows, s, 1:2], stat[0:rows, s, 0:1], 1.0 / DM, EPS,
                                        ALU.mult, ALU.add).then_inc(s_mean, 1)
                dve.wait_ge(s_guess, t + 1)
                rsqrt_newton(nc, dve, stat[0:rows, s, 1:2], stat[0:rows, s, 3:4], stat[0:rows, s, 4:5],
                             stat[0:rows, s, 5:6])
                dve.drain()
                nc.vector.tensor_scalar(x_in[0:rows, s, :], x_in[0:rows, s, :], stat[0:rows, s, 5:6],
                                        None, ALU.mult).then_inc(s_xs, 1)

            def scale_turned(t, s, rows):
                dve.wait_ge(s_xT, t + 1)
                out = xnT[:, :, bass.ds(t * P, P)] if rows == P else xnT[:, :, SEQ:TOK]
                src = acc[s % 2][:, 0:DM].rearrange("p (k t) -> p k t", k=DK)[:, :, 0:rows]
                nc.vector.tensor_tensor(out, src, g_mix[:].unsqueeze(2).broadcast_to([P, DK, rows]),
                                        ALU.mult).then_inc(s_xnT, 1)
            tiles(dve, normalise, scale_turned)

            dve.sem_inc(s_evD, 2)

            def evacuate(c, s, pair, kv, lo):
                dve.wait_ge(s_mm, c + 1)
                dve.wait_ge(s_st[s], pair * 16)
                dve.wait_ge(s_tr, {C_QSB: 2, C_QSW: 10, C_KVSW: 10}[lo] if kv is None or lo == C_KVSW else kv + 1)
                nc.vector.tensor_scalar(stage[:, s, 512:1024], acc[s][:, 512:1024],
                                        SCALE if kv is None else 1.0, None, ALU.mult).then_inc(s_evD, 1)

            def natural(c, s, pair, kv, lo):
                if kv is None:
                    return
                dve.wait_ge(s_tr, kv + 3)
                dve.wait_ge(s_ns[s], (pair - lo // 2) * 32 if lo == C_KV else (C_QSW - C_KV) // 2 * 32)
                nc.vector.tensor_copy(nat[:, s, 0:NT, :], turn[:].rearrange("p (t n) -> p t n", t=NT))
                nc.vector.tensor_copy(nat[0:TS, s, NT, :], acc[s][0:TS, 1152:1280]).then_inc(s_nat, 1)
            columns(dve, [evacuate, natural])

        @block.tensor
        def _(pe):
            pe.wait_ge(s_const, 32)

            def turn_x(t, s, turn, rows):
                pe.wait_ge(s_xs, t + 1)
                pe.wait_ge(s_xnT, t + 1)
                for k in range(DK):
                    last = nc.tensor.transpose(acc[s % 2][:, k * P:k * P + rows], x_in[0:rows, s, k * P:(k + 1) * P],
                                               ident[0:rows, 0:rows])
                last.then_inc(s_xT, 1)
            tiles(pe, turn_x)

            pe.sem_inc(s_tr, 2)
            pe.wait_ge(s_xnT, 2 + NT + 1)

            def project(c, s, pair, kv, lo):
                pe.wait_ge(s_w[s], (pair + 1) * 16)
                pe.wait_ge(s_evA, c + 1)
                pe.wait_ge(s_evD, c + 1)
                if kv is None or lo == C_KVSW:
                    if lo != C_QSB:
                        pe.wait_ge(s_nat, C_QSW - C_KV)
                elif s == 1:
                    pe.wait_ge(s_nat, kv - 1)
                for a, b in ((0, 512), (512, 1024), (SEQ, TOK)):
                    for k in range(DK):
                        last = nc.tensor.matmul(acc[s][:, a:b], w[:, s, k, :], xnT[:, k, a:b],
                                                start=(k == 0), stop=(k == DK - 1))
                last.then_inc(s_mm, 1)

            def turn_natural(c, s, pair, kv, lo):
                if kv is None:
                    return
                pe.wait_ge(s_evA, c + 3)
                pe.wait_ge(s_evD, c + 3)
                pe.wait_ge(s_nat, kv)
                for t in range(NT):
                    nc.tensor.transpose(turn[:, t * P:(t + 1) * P], stage[:, s, t * P:(t + 1) * P], ident[:])
                nc.tensor.transpose(acc[s][0:TS, 1152:1280], stage[:, s, SEQ:TOK], ident[:]).then_inc(s_tr, 1)
            columns(pe, [project, turn_natural])

        @block.gpsimd
        def _(pool):
            def store(c, s, pair, kv, lo):
                pool.wait_ge(s_evA, c + 3)
                pool.wait_ge(s_evD, c + 3)
                pool.dma_start(io["projT"][c, :, :], stage[:, s, :]).then_inc(s_st[s], 16)

            def store_natural(c, s, pair, kv, lo):
                if kv is None:
                    return
                pool.wait_ge(s_nat, kv + 1)
                col = bass.ds(kv * P, P)
                pool.dma_start(io["nat"][0:SEQ, col].rearrange("(t p) n -> p t n", p=P),
                               nat[:, s, 0:NT, :]).then_inc(s_ns[s], 16)
                pool.dma_start(io["nat"][SEQ:TOK, col], nat[0:TS, s, NT, :]).then_inc(s_ns[s], 16)
            columns(pool, [store, store_natural])
            for s in range(2):
                pool.wait_ge(s_st[s], C_END // 2 * 16)
                pool.wait_ge(s_ns[s], NATW // P // 2 * 32)


def attention_phase(nc, io):
    with ExitStack() as ctx:
        sb = lambda name, shape: ctx.enter_context(nc.sbuf_tensor("at_" + name, shape, F32))
        ps = lambda name, shape: ctx.enter_context(nc.psum_tensor("at_" + name, shape, F32))
        sem = lambda name: ctx.enter_context(nc.semaphore(name))

        ident = sb("ident", [P, P])
        neg_suffix = sb("neg_suffix_sb", [P, P])
        neg_ones = sb("neg_ones_sb", [P, P])
        visible = sb("visible_sb", [P, P])
        hidden = sb("hidden_sb", [P, 4 * P])
        alibi = sb("alibi_sb", [P, NH, 2 * P])
        alibi_s = sb("alibi_s", [TS, NH, WIN + TS])
        sinks = sb("sinks", [P, NH])
        g_out = sb("g_out", [P, DK])
        g_ffn = sb("g_ffn", [P, DM])
        w_out = sb("w_out_sb", [P, DK, DM])
        q_pad = sb("q_pad", [P, 4, 2, P])
        kT = sb("kT", [P, 4, P])
        v_blk = sb("v_blk", [P, SBW])
        soft = sb("soft", [P, DM])
        sp = sb("sp", [P, DM])
        later = sb("later", [P, DM])
        probs = sb("probs", [P, DM])
        qw_pad = sb("qw_pad", [P, 4, 2, P])
        kw = sb("kw", [P, 2, 2 * P])
        vw = sb("vw", [P, 2, P])
        win_s = sb("win_s", [P, 4, 2 * P])
        win_pT = sb("win_pT", [P, DK, P])
        win = sb("win_stat", [P, 6, 4])
        rden = sb("rden", [P, NH])
        merged = sb("merged", [P, DM])
        mergedT = sb("mergedT", [P, DK, P])
        x_res = sb("x_res", [P, DM])
        h = sb("h_sb", [P, DM])
        xn = sb("xn_sb", [P, DM])
        xnT = sb("xnT_sb", [P, DK, P])
        junk = sb("junk", [P, DM])
        stat = sb("tail_stat", [P, 6, 2])
        qs_pad = sb("qs_pad", [P, 4, 2, TS])
        ksT = sb("ksT", [P, 4, TS])
        vs_blk = sb("vs_blk", [TS, SBW])
        cache_k = sb("cache_k", [P, 4, SBW])
        cache_v = sb("cache_v", [P, 4, SBW])
        cache_kT = sb("cache_kT", [P, 4, 4, P])
        qws_pad = sb("qws_pad", [P, 4, 2, TS])
        kws_in = sb("kws_in", [P, 2, 2, HD])
        kws = sb("kws", [P, 2, WIN + TS])
        vws = sb("vws", [P, 2, P])

        z = ps("z", [P, 4 * 512])
        o_sb = ps("o_sb", [P, 512])
        wide = ps("wide", [P, 1024])
        o_sw = ps("o_sw", [P, 512])

        names = """const late_const w_out zeroed q qs_in k v vs_in ks_in z ln sp tri a pv sw_in bias
                   zs nm p tp pTe pvw msw ssq mean2 guess2 mA mB tm mTe op h ssh meanh guessh
                   xn tx xTe x_in h_out xn_out xT_out
                   ck cv tk ckT cz cln csp ctri ca cpv kws_turn kws_copied copies""".split()
        S = {n: sem("a_" + n) for n in names}
        block = ctx.enter_context(nc.Block())

        def tiles(engine, step):
            for t in range(3):
                step(t, t)
            with engine.Fori(3, NT) as t:
                step(t, 3)

        def key_block(engine, t, j, n, step):
            step(engine.snap(n), t, j)
            engine.reg_add(n, n, 1)

        def older_blocks(engine, t, past, n, step):
            if past == 3:
                with engine.Fori(2, t) as back:
                    key_block(engine, t, t - 1 - back, n, step)

        def counter(engine):
            n = engine.alloc_register("pairs_" + str(engine.engine).split(".")[-1])
            engine.reg_mov(n, 0)
            return n

        @block.sync
        def _(sync):
            loads = ((ident[:], io["ident"]), (neg_suffix[:], io["neg_suffix"]), (neg_ones[:], io["neg_ones"]),
                     (visible[:], io["visible"]), (hidden[:], io["hidden"]))
            for dst, src in loads:
                sync.dma_start(dst, src).then_inc(S["const"], 16)
            loads = ((alibi[:].rearrange("p h k -> p (h k)"), io["alibi"][0]),
                     (alibi_s[:].rearrange("p h k -> p (h k)"), io["alibi_sample"]),
                     (sinks[:], io["swa_sinks"].partition_broadcast(P)),
                     (g_ffn[:], io["norm_ffn"].partition_broadcast(P)))

            def load_later_constants():
                for dst, src in loads:
                    sync.dma_start(dst, src).then_inc(S["late_const"], 16)
                for k0, g in ((0, "norm_sb_out"), (4, "norm_swa_out")):
                    sync.dma_start(g_out[:, k0:k0 + 4], io[g].rearrange("o (k p) -> p (o k)", p=P),
                                   allow_slow_non_contiguous=True).then_inc(S["late_const"], 16)
                sync.dma_start(w_out[:], io["w_out"].rearrange("(k p) n -> p k n", p=P)).then_inc(S["w_out"], 16)

            sync.wait_ge(S["zeroed"], 4)
            n = counter(sync)

            def load_k(n, t, j):
                hold(sync, S["z"], n + 1)
                j = tile_index(nc, j)
                src = io["projT"][4:8, :, bass.ds(j * P, P)].rearrange("c p t -> p c t")
                sync.dma_start(kT[:], src).then_inc(S["k"], 16)

            def tile(t, past):
                hold(sync, S["z"], sync.snap(n) + 1)
                for half in range(2):
                    rows = slice(half * HD, (half + 1) * HD)
                    src = io["projT"][0:4, rows, bass.ds(t * P, P)].rearrange("c p t -> p c t")
                    sync.dma_start(q_pad[rows, :, half, :], src).then_inc(S["q"], 16)
                hold(sync, S["q"], (t + 1) * 32)
                key_block(sync, t, t, n, load_k)
                if not past:
                    load_later_constants()
                if past:
                    key_block(sync, t, t - 1, n, load_k)
                if past > 1:
                    key_block(sync, t, t - 2, n, load_k)
                older_blocks(sync, t, past, n, load_k)
            tiles(sync, tile)
            for _ in range(2):
                key_block(sync, 0, 0, n, load_k)

            def group(g):
                base = (3 - g) * 512
                hold(sync, S["ckT"], g * 2)
                sync.dma_start(cache_k[:], io["cache_sb_k"][bass.ds(base, 512), :].rearrange(
                    "(b s) c -> s b c", s=P)).then_inc(S["ck"], 16)
                hold(sync, S["cpv"], g + 1)
                sync.dma_start(cache_v[:], io["cache_sb_v"][bass.ds(base, 512), :].rearrange(
                    "(b s) c -> s b c", s=P)).then_inc(S["cv"], 16)
            group(0)
            with sync.Fori(1, 4) as g:
                group(g)

            nat = io["nat"]
            c2 = lambda name: io[name].rearrange("a b s n d -> (a b s) (n d)")
            for dst, src in (
                (c2("sb_k_prompt"), nat[0:SEQ, 0:SBW]), (c2("sb_v_prompt"), nat[0:SEQ, SBW:2 * SBW]),
                (c2("swa_k_prompt"), nat[SEQ - WIN:SEQ, 1024:1152]),
                (c2("swa_v_prompt"), nat[SEQ - WIN:SEQ, 1152:1280]),
                (c2("sb_k_sample"), nat[SEQ:TOK, 0:SBW]), (c2("sb_v_sample"), nat[SEQ:TOK, SBW:2 * SBW]),
                (c2("swa_k_sample")[0:WIN - TS], io["cache_swa_k"][TS:WIN, :]),
                (c2("swa_v_sample")[0:WIN - TS], io["cache_swa_v"][TS:WIN, :]),
                (c2("swa_k_sample")[WIN - TS:WIN], nat[SEQ:TOK, 1024:1152]),
                (c2("swa_v_sample")[WIN - TS:WIN], nat[SEQ:TOK, 1152:1280]),
            ):
                sync.dma_start(dst, src).then_inc(S["copies"], 16)
            sync.wait_ge(S["copies"], 160)

        @block.gpsimd
        def _(pool):
            for t in (q_pad, qw_pad, qs_pad, qws_pad):
                nc.gpsimd.memset(t[:], 0.0).then_inc(S["zeroed"], 1)
            hold(pool, S["zeroed"], 4)
            n = counter(pool)

            def load_v(n, t, j):
                hold(pool, S["pv"], n + 1)
                j = tile_index(nc, j)
                pool.dma_start(v_blk[:], io["nat"][bass.ds(j * P, P), SBW:2 * SBW]).then_inc(S["v"], 16)

            def load_halves(dst, c, t0, n_tok, sem):
                for half in range(2):
                    rows = slice(half * HD, (half + 1) * HD)
                    pool.dma_start(dst[rows, :, half, :], io["projT"][c:c + 4, rows, bass.ds(t0, n_tok)].rearrange(
                        "c p t -> p c t")).then_inc(sem, 16)

            def load_kw(dst, col, t0, n_tok, sem):
                for half in range(2):
                    rows = slice(half * HD, (half + 1) * HD)
                    pool.dma_start(dst[rows, :, col:col + n_tok], io["projT"][C_KVSW, :, bass.ds(t0, n_tok)].rearrange(
                        "(n d) t -> d n t", d=HD)).then_inc(sem, 16)

            def load_sample():
                load_halves(qs_pad, 0, SEQ, TS, S["qs_in"])
                pool.dma_start(ksT[:], io["projT"][4:8, :, SEQ:TOK].rearrange("c p t -> p c t")).then_inc(S["qs_in"], 16)
                pool.dma_start(vs_blk[:], io["nat"][SEQ:TOK, SBW:2 * SBW]).then_inc(S["qs_in"], 16)
                load_halves(qws_pad, C_QSW, SEQ, TS, S["qs_in"])
                for twice in range(2):
                    pool.dma_start(kws_in[:, :, twice, :], io["cache_swa_k"].rearrange(
                        "s (n d) -> s n d", n=2)).then_inc(S["qs_in"], 16)
                load_kw(kws, WIN, SEQ, TS, S["qs_in"])
                pool.dma_start(vws[:, 0, :], io["cache_swa_v"]).then_inc(S["qs_in"], 16)
                pool.dma_start(vws[0:TS, 1, :], io["nat"][SEQ:TOK, 1152:1280]).then_inc(S["qs_in"], 16)

            def store_h(t, rows, tokens):
                hold(pool, S["h"], t + 1)
                pool.dma_start(io["h"][tokens, :], h[0:rows, :]).then_inc(S["h_out"], 16)

            def store_xn(t, rows, tokens):
                hold(pool, S["xn"], t + 1)
                pool.dma_start(io["xn2"][tokens, :], xn[0:rows, :]).then_inc(S["xn_out"], 16)
                hold(pool, S["xTe"], t + 1)
                pool.dma_start(io["xn2T"][t, :, :], xnT[:].rearrange("p k t -> p (k t)")).then_inc(S["xT_out"], 16)

            def tile(t, past):
                hold(pool, S["zs"], t * 2)
                load_halves(qw_pad, C_QSW, t * P, P, S["sw_in"])
                if not past:
                    load_kw(kw, 0, 0, P, S["sw_in"])
                    load_kw(kw, P, 0, P, S["sw_in"])
                else:
                    load_kw(kw, 0, t * P - P, 2 * P, S["sw_in"])
                hold(pool, S["pvw"], t * 2)
                for b in range(2):
                    row = t * P + (b - 1) * P if past or b else 0
                    pool.dma_start(vw[:, b, :], io["nat"][bass.ds(row, P), 1152:1280]).then_inc(S["sw_in"], 16)
                key_block(pool, t, t, n, load_v)
                if past:
                    store_h(t - 1, P, bass.ds(t * P - P, P))
                hold(pool, S["h"], t)
                pool.dma_start(x_res[:], io["x_prompt"][bass.ds(t * P, P), :]).then_inc(S["x_in"], 16)
                if past:
                    key_block(pool, t, t - 1, n, load_v)
                    if past > 1:
                        key_block(pool, t, t - 2, n, load_v)
                    store_xn(t - 1, P, bass.ds(t * P - P, P))
                else:
                    hold(pool, S["nm"], 2)
                    pool.dma_start(alibi[:].rearrange("p h k -> p (h k)"), io["alibi"][1]).then_inc(S["bias"], 16)
                older_blocks(pool, t, past, n, load_v)
                if past == 2:
                    load_sample()
            tiles(pool, tile)
            store_h(NT - 1, P, slice(SEQ - P, SEQ))
            store_xn(NT - 1, P, slice(SEQ - P, SEQ))

            hold(pool, S["h"], NT)
            pool.dma_start(x_res[0:TS, :], io["x_sample"]).then_inc(S["x_in"], 16)
            store_h(NT, TS, slice(SEQ, TOK))
            store_xn(NT, TS, slice(SEQ, TOK))
            for name in ("h_out", "xn_out", "xT_out"):
                hold(pool, S[name], (NT + 1) * 16)
        N_QS = 12

        @block.scalar
        def _(act):
            act.preload_act_table_set("natural_log_exp_and_others")
            n = counter(act)

            def softplus_part(src, ready, ready_n, done):
                hold(act, ready, ready_n)
                nc.scalar.activation(soft[0:src.shape[0], 0:src.shape[1]], src, ACT.Abs)
                act.drain()
                view = soft[0:src.shape[0], 0:src.shape[1]]
                nc.scalar.activation(view, view, ACT.Exp, scale=-1.0)
                act.drain()
                nc.scalar.activation(view, view, ACT.Ln, bias=1.0).then_inc(done, 1)

            def next_softplus(n):
                act.wait_ge(S["sp"], n)
                softplus_part(z[:, bass.ds((n % 2) * 1024, 1024)], S["z"], n + 2, S["ln"])

            def pair_exp(n):
                act.wait_ge(S["tri"], n + 2)
                hold(act, S["pv"], n + 1)
                nc.scalar.activation(probs[:], z[:, bass.ds((n % 2) * 1024, 1024)], ACT.Exp).then_inc(S["a"], 1)

            def window_exp(u, f, rows, keys):
                act.wait_ge(S["nm"], u + 1)
                for hh in range(4):
                    nc.scalar.activation(win_s[0:rows, hh, 0:keys], win_s[0:rows, hh, 0:keys], ACT.Exp,
                                         bias=win[0:rows, 2, hh:hh + 1], accum_out=win[0:rows, 4, hh:hh + 1])
                nc.scalar.activation(win[0:rows, 5, :], win[0:rows, 3, :], ACT.Exp).then_inc(S["p"], 1)

            def window_turned(u, rows):
                act.wait_ge(S["tp"], u + 1)
                act.wait_ge(S["pvw"], u)
                turned = wide[:].rearrange("p (k t) -> p k t", k=DK)
                if rows == P:
                    nc.scalar.activation(win_pT[:], turned, ACT.Copy).then_inc(S["pTe"], 1)
                else:
                    nc.scalar.activation(win_pT[:, 0:DK:2, 0:rows], turned[:, 0:DK:2, 0:rows], ACT.Copy)
                    nc.scalar.activation(win_pT[0:TS, 1:DK:2, 0:rows], turned[0:TS, 1:DK:2, 0:rows],
                                         ACT.Copy).then_inc(S["pTe"], 1)

            def merged_squares(t, rows):
                act.wait_ge(S["msw"], t + 1)
                nc.scalar.activation(junk[0:rows, 0:512], o_sb[0:rows, :], ACT.Square, accum_out=stat[0:rows, 0, 0:1])
                nc.scalar.activation(junk[0:rows, 512:1024], merged[0:rows, 512:1024], ACT.Square,
                                     accum_out=stat[0:rows, 0, 1:2]).then_inc(S["ssq"], 1)

            def merged_scale(t, rows):
                act.wait_ge(S["mean2"], t + 1)
                rsqrt_guess(nc, act, stat[0:rows, 1, :], stat[0:rows, 2, :], stat[0:rows, 3, :]).then_inc(S["guess2"], 1)
                act.wait_ge(S["mB"], t + 1)
                nc.scalar.activation(merged[0:rows, 0:512], o_sb[0:rows, :], ACT.Copy,
                                     scale=stat[0:rows, 5, 0:1]).then_inc(S["mA"], 1)

            def h_scale(t, rows):
                act.wait_ge(S["h"], t + 1)
                nc.scalar.activation(junk[0:rows, :], h[0:rows, :], ACT.Square,
                                     accum_out=stat[0:rows, 0, 0:1]).then_inc(S["ssh"], 1)
                act.wait_ge(S["meanh"], t + 1)
                rsqrt_guess(nc, act, stat[0:rows, 1, 0:1], stat[0:rows, 2, 0:1],
                            stat[0:rows, 3, 0:1]).then_inc(S["guessh"], 1)

            def xn_turned(t, rows):
                act.wait_ge(S["tx"], t + 1)
                act.wait_ge(S["xT_out"], t * 16)
                turned = wide[:].rearrange("p (k t) -> p k t", k=DK)[:, :, 0:rows]
                if rows == P:
                    nc.scalar.activation(xnT[:], turned, ACT.Copy).then_inc(S["xTe"], 1)
                else:
                    nc.scalar.activation(xnT[:].rearrange("p k (c t) -> p k c t", c=COPIES),
                                         turned.unsqueeze(2).broadcast_to([P, DK, COPIES, TS]),
                                         ACT.Copy).then_inc(S["xTe"], 1)

            def window(u, f, rows, keys):
                window_exp(u, f, rows, keys)
                window_turned(u, rows)

            def tail(t, rows):
                merged_squares(t, rows)
                merged_scale(t, rows)
                h_scale(t, rows)
                xn_turned(t, rows)

            def pair(n, t, j):
                next_softplus(n + 1)
                pair_exp(n)

            def diagonal_beside_tail(n, t, j):
                next_softplus(n + 1)
                merged_squares(t - 1, P)
                merged_scale(t - 1, P)
                pair_exp(n)

            def second_beside_window(n, t, j):
                next_softplus(n + 1)
                window_exp(t * 2 + 1, 1, P, 2 * P)
                pair_exp(n)
                window_turned(t * 2 + 1, P)

            def previous_beside_window(n, t, j):
                next_softplus(n + 1)
                h_scale(t - 1, P)
                window_exp(t * 2, 0, P, 2 * P)
                pair_exp(n)
                window_turned(t * 2, P)
                xn_turned(t - 1, P)

            def tile(t, past):
                if past:
                    key_block(act, t, t, n, diagonal_beside_tail)
                    key_block(act, t, t - 1, n, previous_beside_window)
                else:
                    key_block(act, t, t, n, pair)
                    window(t * 2, 0, P, 2 * P)
                if past > 1:
                    key_block(act, t, t - 2, n, second_beside_window)
                    older_blocks(act, t, past, n, pair)
                else:
                    window(t * 2 + 1, 1, P, 2 * P)
            softplus_part(z[:, 0:1024], S["z"], 2, S["ln"])
            tiles(act, tile)
            tail(NT - 1, P)

            softplus_part(z[0:TS, 0:256], S["cz"], 1, S["cln"])
            act.wait_ge(S["ctri"], 1)
            nc.scalar.activation(probs[0:TS, 0:256], z[0:TS, 0:256], ACT.Exp).then_inc(S["ca"], 1)
            with act.Fori(1, 5) as g:
                act.wait_ge(S["tk"], g * 2 - 1)
                act.wait_ge(S["cz"], g)
                nc.scalar.activation(cache_kT[:, 0:2, :, :].rearrange("p b m s -> p (b m s)"), z[:, 1024:2048],
                                     ACT.Copy).then_inc(S["ckT"], 1)
                softplus_part(z[:, 0:1024], S["cz"], g + 1, S["cln"])
                act.wait_ge(S["ctri"], g + 1)
                act.wait_ge(S["cpv"], g)
                nc.scalar.activation(probs[:], z[:, 0:1024], ACT.Exp).then_inc(S["ca"], 1)
            act.wait_ge(S["kws_turn"], 1)
            act.wait_ge(S["qs_in"], N_QS * 16)
            nc.scalar.activation(kws[:, :, 0:WIN], wide[:, 0:256].rearrange("p (n s) -> p n s", n=2),
                                 ACT.Copy).then_inc(S["kws_copied"], 1)
            for f in range(2):
                window(NT * 2 + f, f, TS, WIN + TS)
            tail(NT, TS)

        @block.vector
        def _(dve):
            dve.wait_ge(S["const"], 5 * 16)
            n = counter(dve)

            def diagonal(n, t, j):
                dve.wait_ge(S["tri"], n + 1)
                nc.vector.memset(later[:], 0.0)
                dve.wait_ge(S["ln"], n + 1)
                nc.vector.scalar_tensor_tensor(sp[:], z[:, bass.ds((n % 2) * 1024, 1024)], 0.0, soft[:],
                                               ALU.max, ALU.add)
                dve.drain()
                view = sp[:].rearrange("p (h q) -> p h q", h=NH)
                nc.vector.tensor_tensor(view, view, visible[:].unsqueeze(1).broadcast_to([P, NH, P]),
                                        ALU.mult).then_inc(S["sp"], 1)

            def earlier(n, t, j):
                dve.wait_ge(S["tri"], n + 1)
                nc.vector.tensor_tensor(later[:], later[:], sp[:], ALU.add)
                dve.drain()
                dve.wait_ge(S["ln"], n + 1)
                nc.vector.scalar_tensor_tensor(sp[:], z[:, bass.ds((n % 2) * 1024, 1024)], 0.0, soft[:],
                                               ALU.max, ALU.add).then_inc(S["sp"], 1)

            def window_max(u, f, rows, keys, bias):
                dve.wait_ge(S["zs"], u + 1)
                dve.wait_ge(S["tp"], u)
                scores = win_s[0:rows, :, 0:keys]
                nc.vector.tensor_tensor(scores, wide[0:rows, :].rearrange("p (h k) -> p h k", h=4)[:, :, 0:keys],
                                        bias, ALU.add)
                dve.drain()
                nc.vector.tensor_reduce(win[0:rows, 0, :], scores, AXX, ALU.max)
                dve.drain()
                nc.vector.tensor_tensor(win[0:rows, 1, :], win[0:rows, 0, :], sinks[0:rows, 4 * f:4 * f + 4], ALU.max)
                dve.drain()
                nc.vector.tensor_tensor(win[0:rows, 3, :], sinks[0:rows, 4 * f:4 * f + 4], win[0:rows, 1, :],
                                        ALU.subtract)
                nc.vector.tensor_scalar(win[0:rows, 2, :], win[0:rows, 1, :], -1.0, None, ALU.mult).then_inc(S["nm"], 1)

            def window_sum(u, f, rows):
                dve.wait_ge(S["p"], u + 1)
                nc.vector.tensor_tensor(win[0:rows, 4, :], win[0:rows, 4, :], win[0:rows, 5, :], ALU.add)
                dve.drain()
                nc.vector.reciprocal(rden[0:rows, 4 * f:4 * f + 4], win[0:rows, 4, :])

            def merge_window(t, rows, n):
                hold(dve, S["pvw"], t * 2 + 2)
                hold(dve, S["pv"] if rows == P else S["cpv"], n + 1 if rows == P else 5)
                dve.drain()
                nc.vector.tensor_tensor(
                    merged[0:rows, 512:1024].rearrange("p (h d) -> p h d", h=NH),
                    o_sw[0:rows, :].rearrange("p (h d) -> p h d", h=NH),
                    rden[0:rows, :].unsqueeze(2).broadcast_to([rows, NH, HD]), ALU.mult).then_inc(S["msw"], 1)

            def merged_scale(t, rows):
                dve.wait_ge(S["ssq"], t + 1)
                nc.vector.tensor_scalar(stat[0:rows, 1, :], stat[0:rows, 0, :], 1.0 / 512, EPS,
                                        ALU.mult, ALU.add).then_inc(S["mean2"], 1)
                dve.wait_ge(S["guess2"], t + 1)
                rsqrt_newton(nc, dve, stat[0:rows, 1, :], stat[0:rows, 3, :], stat[0:rows, 4, :], stat[0:rows, 5, :])
                dve.drain()
                nc.vector.tensor_scalar(merged[0:rows, 512:1024], merged[0:rows, 512:1024], stat[0:rows, 5, 1:2],
                                        None, ALU.mult).then_inc(S["mB"], 1)

            def merged_turned(t, rows):
                dve.wait_ge(S["tm"], t + 1)
                nc.vector.tensor_tensor(mergedT[:, :, 0:rows],
                                        wide[:].rearrange("p (k t) -> p k t", k=DK)[:, :, 0:rows],
                                        g_out[:].unsqueeze(2).broadcast_to([P, DK, rows]), ALU.mult).then_inc(S["mTe"], 1)

            def residual(t, rows):
                dve.wait_ge(S["op"], t + 1)
                dve.wait_ge(S["x_in"], t * 16 + 16)
                dve.wait_ge(S["h_out"], t * 16)
                nc.vector.tensor_tensor(h[0:rows, :], wide[0:rows, :], x_res[0:rows, :], ALU.add).then_inc(S["h"], 1)

            def h_mean(t, rows):
                dve.wait_ge(S["ssh"], t + 1)
                nc.vector.tensor_scalar(stat[0:rows, 1, 0:1], stat[0:rows, 0, 0:1], 1.0 / DM, EPS,
                                        ALU.mult, ALU.add).then_inc(S["meanh"], 1)

            def h_scale(t, rows):
                dve.wait_ge(S["guessh"], t + 1)
                rsqrt_newton(nc, dve, stat[0:rows, 1, 0:1], stat[0:rows, 3, 0:1], stat[0:rows, 4, 0:1],
                             stat[0:rows, 5, 0:1])
                dve.drain()
                dve.wait_ge(S["xn_out"], t * 16)
                nc.vector.scalar_tensor_tensor(xn[0:rows, :], h[0:rows, :], stat[0:rows, 5, 0:1], g_ffn[0:rows, :],
                                               ALU.mult, ALU.mult).then_inc(S["xn"], 1)

            def window(u, f, rows, keys, bias):
                window_max(u, f, rows, keys, bias)
                window_sum(u, f, rows)

            def tail(t, rows, n):
                merge_window(t, rows, n)
                merged_scale(t, rows)
                merged_turned(t, rows)
                residual(t, rows)
                h_mean(t, rows)
                h_scale(t, rows)

            def bias(f):
                return alibi[:, 4 * f:4 * f + 4, :]

            def diagonal_beside_tail(n, t, j):
                diagonal(n, t, j)
                merge_window(t - 1, P, n)
                merged_scale(t - 1, P)
                merged_turned(t - 1, P)

            def second_beside_window(n, t, j):
                earlier(n, t, j)
                window(t * 2 + 1, 1, P, 2 * P, bias(1))

            def previous_beside_window(n, t, j):
                earlier(n, t, j)
                residual(t - 1, P)
                h_mean(t - 1, P)
                window_max(t * 2, 0, P, 2 * P, bias(0))
                h_scale(t - 1, P)
                window_sum(t * 2, 0, P)

            def tile(t, past):
                if past:
                    dve.wait_ge(S["bias"], 16)
                    key_block(dve, t, t, n, diagonal_beside_tail)
                    key_block(dve, t, t - 1, n, previous_beside_window)
                else:
                    key_block(dve, t, t, n, diagonal)
                    dve.wait_ge(S["late_const"], 6 * 16)
                    window(t * 2, 0, P, 2 * P, bias(0))
                if past > 1:
                    key_block(dve, t, t - 2, n, second_beside_window)
                    older_blocks(dve, t, past, n, earlier)
                else:
                    window(t * 2 + 1, 1, P, 2 * P, bias(1))
            tiles(dve, tile)
            tail(NT - 1, P, dve.snap(n))

            nc.vector.memset(later[:], 0.0)
            dve.drain()
            dve.wait_ge(S["cln"], 1)
            nc.vector.scalar_tensor_tensor(sp[0:TS, 0:256], z[0:TS, 0:256], 0.0, soft[0:TS, 0:256], ALU.max, ALU.add)
            dve.drain()
            view = sp[0:TS, 0:256].rearrange("p (h q) -> p h q", h=NH)
            own = visible[0:TS, 0:TS].unsqueeze(1).broadcast_to([TS, NH, TS])
            nc.vector.tensor_tensor(view, view, own, ALU.mult).then_inc(S["csp"], 1)
            dve.drain()
            nc.vector.tensor_copy(later[0:TS, 0:256], sp[0:TS, 0:256])
            dve.drain()
            with dve.Fori(1, 5) as g:
                dve.wait_ge(S["tk"], g * 2)
                dve.wait_ge(S["cz"], g)
                nc.vector.tensor_copy(cache_kT[:, 2:4, :, :].rearrange("p b m s -> p (b m s)"),
                                      wide[:]).then_inc(S["ckT"], 1)
                dve.wait_ge(S["ctri"], g)
                dve.wait_ge(S["cln"], g + 1)
                nc.vector.scalar_tensor_tensor(sp[:], z[:, 0:1024], 0.0, soft[:], ALU.max, ALU.add).then_inc(S["csp"], 1)
                hold(dve, S["ctri"], g + 1)
                for b in range(4):
                    dve.drain()
                    nc.vector.tensor_tensor(later[:, 0:256], later[:, 0:256], sp[:, b * 256:(b + 1) * 256], ALU.add)
                dve.drain()
            for f in range(2):
                window(NT * 2 + f, f, TS, WIN + TS, alibi_s[:, 4 * f:4 * f + 4, :])
            tail(NT, TS, 0)

        @block.tensor
        def _(pe):
            pe.wait_ge(S["const"], 5 * 16)
            n = counter(pe)

            def scores(n):
                pe.wait_ge(S["k"], n * 16 + 16)
                for m in range(4):
                    last = nc.tensor.matmul(z[:, bass.ds((n % 2) * 1024 + m * 256, 256)], kT[:, m, :],
                                            q_pad[:, m, :, :].rearrange("p a q -> p (a q)"),
                                            start=(m % 2 == 0), stop=False, skip_group_check=True)
                last.then_inc(S["z"], 1)

            def sums(n, diagonal):
                pe.wait_ge(S["sp"], n + 1)
                for b in range(2):
                    out = z[:, bass.ds((n % 2) * 1024 + b * 512, 512)]
                    cols = slice(b * 512, (b + 1) * 512)
                    nc.tensor.matmul(out, neg_suffix[:], sp[:, cols], start=False, stop=False, skip_group_check=True)
                    if diagonal:
                        last = nc.tensor.matmul(out, ident[:], hidden[:], start=False, stop=True,
                                                skip_group_check=True)
                    else:
                        last = nc.tensor.matmul(out, neg_ones[:], later[:, cols], start=False, stop=True,
                                                skip_group_check=True)
                last.then_inc(S["tri"], 1)

            def values(n, diagonal):
                pe.wait_ge(S["a"], n + 1)
                pe.wait_ge(S["v"], n * 16 + 16)
                for hd in range(NH):
                    last = nc.tensor.matmul(o_sb[:, hd * HD:(hd + 1) * HD], probs[:, hd * P:(hd + 1) * P],
                                            v_blk[:, hd * HD:(hd + 1) * HD], start=(diagonal and hd == 0),
                                            stop=False, skip_group_check=True)
                last.then_inc(S["pv"], 1)

            def window_scores(f, rows, width, queries, keys):
                for hh in range(4):
                    hd = 4 * f + hh
                    last = nc.tensor.matmul(wide[0:rows, hh * 256:hh * 256 + width], queries[:, hd // 2, hd % 2, :],
                                            keys[:, f, 0:width], start=(hh % 2 == 0), stop=True, skip_group_check=True)
                last.then_inc(S["zs"], 1)

            def window_turn(u, rows, blocks):
                pe.wait_ge(S["p"], u + 1)
                for hh in range(4):
                    for b, size in enumerate(blocks):
                        i = 2 * hh + b
                        last = nc.tensor.transpose(wide[0:size, i * P:i * P + rows],
                                                   win_s[0:rows, hh, b * P:b * P + size], ident[0:rows, 0:rows])
                last.then_inc(S["tp"], 1)

            def window_values(u, f, rows, blocks, values):
                pe.wait_ge(S["pTe"], u + 1)
                for hh in range(4):
                    hd = 4 * f + hh
                    for b, size in enumerate(blocks):
                        last = nc.tensor.matmul(o_sw[0:rows, hd * HD:(hd + 1) * HD],
                                                win_pT[0:size, 2 * hh + b, 0:rows],
                                                values[0:size, b, f * HD:(f + 1) * HD],
                                                start=(hd == 0 and b == 0), stop=False, skip_group_check=True)
                last.then_inc(S["pvw"], 1)

            def merged_turn(t, rows):
                pe.wait_ge(S["mA"], t + 1)
                pe.wait_ge(S["mB"], t + 1)
                for k in range(DK):
                    last = nc.tensor.transpose(wide[:, k * P:k * P + rows], merged[0:rows, k * P:(k + 1) * P],
                                               ident[0:rows, 0:rows])
                last.then_inc(S["tm"], 1)

            def project(t, rows):
                pe.wait_ge(S["mTe"], t + 1)
                for k in range(DK):
                    for b in range(2):
                        last = nc.tensor.matmul(wide[0:rows, b * 512:(b + 1) * 512], mergedT[:, k, 0:rows],
                                                w_out[:, k, b * 512:(b + 1) * 512], start=(k == 0),
                                                stop=(k == DK - 1), skip_group_check=True)
                last.then_inc(S["op"], 1)

            def xn_turn(t, rows):
                pe.wait_ge(S["xn"], t + 1)
                for k in range(DK):
                    last = nc.tensor.transpose(wide[:, k * P:k * P + rows], xn[0:rows, k * P:(k + 1) * P],
                                               ident[0:rows, 0:rows])
                last.then_inc(S["tx"], 1)

            def window(u, f, rows, blocks, queries, keys, values):
                window_scores(f, rows, sum(blocks), queries, keys)
                window_turn(u, rows, blocks)
                window_values(u, f, rows, blocks, values)

            def tail(t, rows):
                merged_turn(t, rows)
                project(t, rows)
                xn_turn(t, rows)

            def pair(n, diagonal):
                sums(n, diagonal)
                values(n, diagonal)
                scores(n + 2)

            def diagonal_beside_tail(n, t, j):
                sums(n, True)
                merged_turn(t - 1, P)
                values(n, True)
                scores(n + 2)
                project(t - 1, P)

            def previous_beside_window(n, t, j):
                sums(n, False)
                pe.wait_ge(S["sw_in"], t * 96 + 128)
                pe.wait_ge(S["h"], t)
                window_scores(0, P, 2 * P, qw_pad, kw)
                values(n, False)
                window_turn(t * 2, P, (P, P))
                scores(n + 2)
                window_values(t * 2, 0, P, (P, P), vw)
                xn_turn(t - 1, P)

            def second_beside_window(n, t, j):
                sums(n, False)
                pe.wait_ge(S["xTe"], t)
                window_scores(1, P, 2 * P, qw_pad, kw)
                values(n, False)
                window_turn(t * 2 + 1, P, (P, P))
                scores(n + 2)
                window_values(t * 2 + 1, 1, P, (P, P), vw)

            for name in ("z", "tri", "pv"):
                pe.sem_inc(S[name], 1)
            scores(0)
            scores(1)

            def tile(t, past):
                if past:
                    pe.wait_ge(S["w_out"], 16)
                    key_block(pe, t, t, n, diagonal_beside_tail)
                    key_block(pe, t, t - 1, n, previous_beside_window)
                else:
                    key_block(pe, t, t, n, lambda n, t, j: pair(n, True))
                    pe.wait_ge(S["sw_in"], 8 * 16)
                    window(t * 2, 0, P, (P, P), qw_pad, kw, vw)
                if past > 1:
                    key_block(pe, t, t - 2, n, second_beside_window)
                    older_blocks(pe, t, past, n, lambda n, t, j: pair(n, False))
                else:
                    pe.wait_ge(S["xTe"], t)
                    window(t * 2 + 1, 1, P, (P, P), qw_pad, kw, vw)
            tiles(pe, tile)
            tail(NT - 1, P)

            pe.wait_ge(S["qs_in"], N_QS * 16)
            pe.wait_ge(S["ln"], NT * (NT + 1) // 2 + 1)
            for m in range(4):
                last = nc.tensor.matmul(z[0:TS, m * 64:m * 64 + 64], ksT[:, m, :],
                                        qs_pad[:, m, :, :].rearrange("p a q -> p (a q)"),
                                        start=(m == 0), stop=False, skip_group_check=True)
            last.then_inc(S["cz"], 1)
            pe.wait_ge(S["csp"], 1)
            nc.tensor.matmul(z[0:TS, 0:256], neg_suffix[0:TS, 0:TS], sp[0:TS, 0:256], start=False, stop=False,
                             skip_group_check=True)
            for b in range(2):
                last = nc.tensor.matmul(z[0:TS, b * P:(b + 1) * P], ident[0:TS, 0:TS],
                                        hidden[0:TS, :].rearrange("p (r q) -> p r q", r=4)[:, :, 0:TS],
                                        start=False, stop=True, skip_group_check=True)
            last.then_inc(S["ctri"], 1)
            pe.wait_ge(S["ca"], 1)
            for hd in range(NH):
                last = nc.tensor.matmul(o_sb[0:TS, hd * HD:(hd + 1) * HD], probs[0:TS, hd * TS:(hd + 1) * TS],
                                        vs_blk[:, hd * HD:(hd + 1) * HD], start=(hd == 0), stop=False,
                                        skip_group_check=True)
            last.then_inc(S["cpv"], 1)
            with pe.Fori(1, 5) as g:
                pe.wait_ge(S["ck"], g * 16)
                for b in range(4):
                    dst = z[:, 1024 + b * 512:1536 + b * 512] if b < 2 else wide[:, (b - 2) * 512:(b - 1) * 512]
                    for m in range(4):
                        last = nc.tensor.transpose(dst[:, m * P:(m + 1) * P], cache_k[:, b, m * P:(m + 1) * P], ident[:])
                    if b % 2:
                        last.then_inc(S["tk"], 1)
                pe.wait_ge(S["ckT"], g * 2)
                for b in range(4):
                    for m in range(4):
                        last = nc.tensor.matmul(z[:, b * 256 + m * 64:b * 256 + m * 64 + 64], cache_kT[:, b, m, :],
                                                qs_pad[:, m, :, :].rearrange("p a q -> p (a q)"),
                                                start=(m == 0 and b % 2 == 0), stop=False, skip_group_check=True)
                last.then_inc(S["cz"], 1)
                pe.wait_ge(S["csp"], g + 1)
                for b in range(4):
                    out = z[:, b * 256:(b + 1) * 256]
                    nc.tensor.matmul(out, neg_suffix[:], sp[:, b * 256:(b + 1) * 256], start=False, stop=False,
                                     skip_group_check=True)
                    for b2 in range(b + 1, 4):
                        nc.tensor.matmul(out, neg_ones[:], sp[:, b2 * 256:(b2 + 1) * 256], start=False, stop=False,
                                         skip_group_check=True)
                    last = nc.tensor.matmul(out, neg_ones[:], later[:, 0:256], start=False, stop=True,
                                            skip_group_check=True)
                last.then_inc(S["ctri"], 1)
                pe.wait_ge(S["ca"], g + 1)
                pe.wait_ge(S["cv"], g * 16)
                for b in range(4):
                    for hd in range(NH):
                        last = nc.tensor.matmul(o_sb[0:TS, hd * HD:(hd + 1) * HD],
                                                probs[:, b * 256 + hd * TS:b * 256 + (hd + 1) * TS],
                                                cache_v[:, b, hd * HD:(hd + 1) * HD], start=False, stop=False,
                                                skip_group_check=True)
                last.then_inc(S["cpv"], 1)
            for kv in range(2):
                last = nc.tensor.transpose(wide[:, kv * P:(kv + 1) * P],
                                           kws_in[:, kv, :, :].rearrange("p a d -> p (a d)"), ident[:])
            last.then_inc(S["kws_turn"], 1)
            pe.wait_ge(S["kws_copied"], 1)
            for f in range(2):
                window(NT * 2 + f, f, TS, (WIN, TS), qws_pad, kws, vws)
            tail(NT, TS)


def expert_phase(nc, io):
    with ExitStack() as ctx:
        def sb(name, shape, dt=F32):
            return ctx.enter_context(nc.sbuf_tensor("ex_" + name, shape, dt))
        ps = lambda name, shape: ctx.enter_context(nc.psum_tensor("ex_" + name, shape, F32))
        sem = lambda name: ctx.enter_context(nc.semaphore("e_" + name))

        ident = sb("ident", [P, P])
        fold = sb("fold", [P, TS])
        iota = sb("iota", [P, NCAND])
        g_final = sb("g_final", [P, DM])
        w_q = sb("w_q", [P, DK, PH * 2 * QH])
        keys = sb("keys", [P, 2, QH])
        keysT = sb("keysT", [P, 2, NKEY])
        xT_first = sb("xT_first", [P, DK, P])
        xT = sb("xT", [P, DK, P])
        q = sb("q", [P, 2 * QH])
        qT = sb("qT", [P, 2, P])
        cut = sb("cut", [P, 2, NKEY])
        val = sb("val", [P, 2, TOPK])
        ind = sb("ind", [P, 2, TOPK], U32)
        indf = sb("indf", [P, 2, TOPK])
        row = sb("row", [P, TOPK])
        cand = sb("cand", [P, 2, NCAND])
        cand_cut = sb("cand_cut", [P, NCAND])
        best = sb("best", [P, TOPK])
        pos = sb("pos", [P, TOPK], U32)
        posf = sb("posf", [P, TOPK])
        pick = sb("pick", [P, TOPK, NCAND])
        idxf = sb("idxf", [P, TOPK])
        gate = sb("gate", [P, TOPK])
        soft = sb("soft", [P, 3])
        idx_all = sb("idx_all", [P, (NT + 1) * SLOTS], U32)
        gate_all = sb("gate_all", [P, (NT + 1) * SLOTS])
        idx = sb("idx", [P, 2, TOPK], U32)
        idx_sample = sb("idx_sample", [P, 2, TOPK], U32)
        u_row = sb("u_row", [P, RING, DM])
        v_row = sb("v_row", [P, RING, DM])
        hid = sb("hid", [P, 2, TOPK])
        act_hid = sb("act_hid", [P, 2, TOPK])
        weight = sb("weight", [P, 2, TOPK])
        diag = sb("diag", [P, 2, TOPK, P])
        x_tok = sb("x_tok", [P, DM])
        h = sb("h", [P, DM])
        y = sb("y", [P, DM])
        y_out = sb("y_out", [P, DM])
        stat = sb("stat", [P, 6])

        y_acc = ps("y_acc", [P, DM])
        x_ps = ps("x_ps", [P, DM])
        q_ps = ps("q_ps", [P, 512])
        qT_ps = ps("qT_ps", [P, 512])
        s_ps = ps("s_ps", [P, 1024])

        names = """idx shared xT_first w_q_first w_q const keys_turn keys_copied xT q qe qt qTe scores best gate_exp routed
                   dot gelu weight diag vmm x_in x_ps h_in y_zero y squares mean guess y_out y_stored""".split()
        S = {n: sem(n) for n in names}
        S_U = [sem(f"u_row{i}") for i in range(RING)]
        S_V = [sem(f"v_row{i}") for i in range(RING)]
        DOT0 = RING
        VMM0 = RING + TOPK
        block = ctx.enter_context(nc.Block())

        def tiles(engine, tile):
            tile(0, P)
            with engine.Fori(1, NT) as t:
                tile(t, P)
            tile(NT, TS)

        def units(engine, t, rows, unit):
            if rows == TS:
                for e in range(2):
                    unit(t * PH + e, e, [], e == 0)
            elif isinstance(t, int):
                def both(head):
                    return [(2 * head + 1, head + 1, xT_first, head + 1, 0), (2 * head + 2, head + PH, xT, head, 1)]
                with engine.Fori(0, PH // 2 - 1) as pair:
                    for e in range(2):
                        unit(pair * 2 + e, e, both(pair * 2 + e), False)
                unit(PH - 2, 0, both(PH - 2), False)
                unit(PH - 1, 1, [(2 * PH - 1, 2 * PH - 1, xT, PH - 1, 0)], False)
            else:
                def two(pair, opens):
                    for e in range(2):
                        head = pair * 2 + e
                        unit(t * PH + head, e, [(t * PH + head + PH, t * PH + head + PH, xT, head, 0)],
                             opens and e == 0)
                two(0, True)
                with engine.Fori(1, PH // 2) as pair:
                    two(pair, False)

        def share(table, e, c):
            per_head = table[c * TS:(c + 1) * TS, NT * SLOTS:].rearrange("p (h k) -> p h k", h=PH)
            return per_head[:, 4 * e:4 * e + 4, c * PART:(c + 1) * PART]

        def shared(table, e, c):
            return table[c * TS:(c + 1) * TS, e, :].rearrange("p (h k) -> p h k", h=4)

        @block.sync
        def _(sync):
            for dst, src in ((ident[:], io["ident"]), (fold[:], io["fold"]), (iota[:], io["rank_iota"]),
                             (g_final[:], io["norm_final"].partition_broadcast(P)),
                             (keys[:, 0, :], io["peer_keys_1"]), (keys[:, 1, :], io["peer_keys_2"])):
                sync.dma_start(dst, src).then_inc(S["const"], 16)
            for cols in (slice(0, 2 * QH), slice(2 * QH, 2 * PH * QH)):
                sync.dma_start(w_q[:, :, cols], io["w_peer_q"].rearrange("(k p) n -> p k n", p=P)[:, :, cols]
                               ).then_inc(S["w_q" if cols.start else "w_q_first"], 16)
                if cols.start == 0:
                    sync.dma_start(xT_first[:].rearrange("p k t -> p (k t)"), io["xn2T"][0, :, :]
                                   ).then_inc(S["xT_first"], 16)

            def load_xT(t):
                if not (isinstance(t, int) and t == 1):
                    hold(sync, S["q"], t * PH)
                sync.dma_start(xT[:].rearrange("p k t -> p (k t)"), io["xn2T"][t, :, :]).then_inc(S["xT"], 16)

            def load_x(t, rows, tokens):
                hold(sync, S["x_ps"], t)
                for first in range(0, P, rows):
                    sync.dma_start(x_tok[first:first + rows, :], io["xn2"][tokens, :]).then_inc(S["x_in"], 16)

            def load_h(t, rows, tokens):
                if not isinstance(t, int) or t > 0:
                    hold(sync, S["y_stored"], t * 16)
                sync.dma_start(h[0:rows, :], io["h"][tokens, :]).then_inc(S["h_in"], 16)

            def store(t, rows, dst):
                hold(sync, S["y_out"], t + 1)
                sync.dma_start(dst, y_out[0:rows, :]).then_inc(S["y_stored"], 16)

            prompt = io["y_prompt"].rearrange("a t d -> (a t) d")
            load_x(0, P, slice(0, P))
            load_xT(1)
            load_h(0, P, slice(0, P))
            with sync.Fori(1, NT) as t:
                load_x(t, P, bass.ds(t * P, P))
                load_xT(t + 1)
                store(t - 1, P, prompt[bass.ds(t * P - P, P), :])
                load_h(t, P, bass.ds(t * P, P))
            load_x(NT, TS, slice(SEQ, TOK))
            store(NT - 1, P, prompt[SEQ - P:SEQ, :])
            load_h(NT, TS, slice(SEQ, TOK))
            store(NT, TS, io["y_sample"].rearrange("a t d -> (a t) d"))
            sync.wait_ge(S["y_stored"], (NT + 1) * 16)

        @block.gpsimd
        def _(pool):
            def experts(u, e, routed):
                hold(pool, S["routed"], routed)
                nc.gpsimd.tensor_copy(idx[:, e, :], idx_all[:, bass.ds(u * TOPK, TOPK)]).then_inc(S["idx"], 1)
                hold(pool, S["idx"], u + 1)

            def gather_u(u, rows_of, e, k):
                hold(pool, S["dot"], u * TOPK + (k + 1 + DOT0 - RING))
                pool.indirect_dma_start(u_row[:, k % RING, :], None, io["peer_u"],
                                        bass.IndirectOffsetOnAxis(ap=rows_of[:, e, k:k + 1], axis=0),
                                        ).then_inc(S_U[k % RING], 16)

            def gather_v(u, rows_of, e, k):
                hold(pool, S["vmm"], u * TOPK + (k + 1 + VMM0 - RING))
                pool.indirect_dma_start(v_row[:, k % RING, :], None, io["peer_v"],
                                        bass.IndirectOffsetOnAxis(ap=rows_of[:, e, k:k + 1], axis=0),
                                        ).then_inc(S_V[k % RING], 16)

            def unit(u, e, table, next_table, next_routed):
                for k in range(RING, TOPK):
                    gather_u(u, table, e, k)
                for k in range(RING):
                    gather_v(u, table, e, k)
                if next_table is idx:
                    experts(u + 1, 1 - e, next_routed)
                elif next_table is idx_sample:
                    hold(pool, S["shared"], 1)
                for k in range(RING, TOPK):
                    gather_v(u, table, e, k)
                    if next_table is not None:
                        gather_u(u + 1, next_table, 1 - e, k - RING)

            experts(0, 0, 2)
            for k in range(RING):
                gather_u(0, idx, 0, k)
            with pool.Fori(0, PH // 2) as pair:
                for e in range(2):
                    unit(pair * 2 + e, e, idx, idx, 2 * (pair * 2 + e + 1) + 1)
            with pool.Fori(PH // 2, NT * PH // 2 - 1) as pair:
                for e in range(2):
                    unit(pair * 2 + e, e, idx, idx, pair * 2 + e + 3)
            unit(NT * PH - 2, 0, idx, idx, NT * PH + 1)
            unit(NT * PH - 1, 1, idx, idx_sample, None)
            unit(NT * PH, 0, idx_sample, idx_sample, None)
            unit(NT * PH + 1, 1, idx_sample, None, None)

        @block.scalar
        def _(act):
            def route_queries(m):
                act.wait_ge(S["q"], m + 1)
                nc.scalar.activation(q[:], q_ps[:, 0:2 * QH], ACT.Copy).then_inc(S["qe"], 1)
                act.wait_ge(S["qt"], m + 1)
                nc.scalar.activation(qT[:].rearrange("p f t -> p (f t)"), qT_ps[:, 0:2 * P],
                                     ACT.Copy).then_inc(S["qTe"], 1)

            def route_gates(m):
                act.wait_ge(S["best"], m + 1)
                nc.scalar.activation(gate[:], best[:], ACT.Exp, bias=soft[:, 0:1],
                                     accum_out=soft[:, 1:2]).then_inc(S["gate_exp"], 1)

            act.sem_inc(S["qe"], 1)
            act.wait_ge(S["keys_turn"], 1)
            nc.scalar.activation(keysT[:].rearrange("p f n -> p (f n)"), qT_ps[:, 0:2 * NKEY],
                                 ACT.Copy).then_inc(S["keys_copied"], 1)
            route_queries(0)
            route_gates(0)

            def finish(t, rows):
                act.wait_ge(S["y"], t + 1)
                nc.scalar.activation(y_out[0:rows, :], y[0:rows, :], ACT.Square,
                                     accum_out=stat[0:rows, 0:1]).then_inc(S["squares"], 1)
                act.wait_ge(S["mean"], t + 1)
                rsqrt_guess(nc, act, stat[0:rows, 1:2], stat[0:rows, 2:3], stat[0:rows, 3:4]).then_inc(S["guess"], 1)

            def tile(t, rows):
                act.wait_ge(S["x_in"], t * 16 + (16 if rows == P else 16 * COPIES))
                act.wait_ge(S["dot"], t * SLOTS + DOT0)
                nc.scalar.activation(x_ps[:], x_tok[:], ACT.Copy).then_inc(S["x_ps"], 1)

                def unit(u, e, routes, opens):
                    for r, *_ in routes:
                        route_queries(r)
                    if opens:
                        finish(t - 1, P)
                    act.wait_ge(S["dot"], u * TOPK + (TOPK + DOT0))
                    nc.scalar.activation(act_hid[:, e, :], hid[:, e, :], ACT.Gelu).then_inc(S["gelu"], 1)
                    act.wait_ge(S["vmm"], u * TOPK + (VMM0 - TOPK))
                    act.wait_ge(S["weight"], u + 1)
                    for k in range(TOPK):
                        made = nc.scalar.activation(diag[:, e, k, 0:rows], (ident if rows == P else fold)[:], ACT.Copy,
                                                    scale=weight[:, e, k:k + 1])
                        if k % 4 == 3:
                            made.then_inc(S["diag"], 1)
                    for r, *_ in routes:
                        route_gates(r)
                units(act, t, rows, unit)
            tiles(act, tile)
            finish(NT, TS)

        @block.vector
        def _(dve):
            dve.sem_inc(S["dot"], DOT0)
            dve.sem_inc(S["routed"], 1)
            dve.wait_ge(S["const"], 6 * 16)

            def top16(values, rest, out, where):
                for v, o in zip(values, out):
                    nc.vector.max(o[:, 0:8], v)
                dve.drain()
                for v, r, o, w in zip(values, rest, out, where):
                    nc.vector.max_index(w[:, 0:8], o[:, 0:8], v)
                    nc.vector.match_replace(r, o[:, 0:8], v, LOWEST)
                dve.drain()
                for r, o in zip(rest, out):
                    nc.vector.max(o[:, 8:16], r)
                dve.drain()
                for r, o, w in zip(rest, out, where):
                    nc.vector.max_index(w[:, 8:16], o[:, 8:16], r)
                dve.drain()

            def route(m, u, bank):
                hold(dve, S["scores"], m + 1)
                scores = s_ps[:, bank * 512:bank * 512 + 2 * NKEY]
                top16([scores[:, f * NKEY:(f + 1) * NKEY] for f in range(2)], [cut[:, f, :] for f in range(2)],
                      [val[:, f, :] for f in range(2)], [ind[:, f, :] for f in range(2)])
                nc.vector.tensor_copy(indf[:], ind[:])
                dve.drain()
                nc.vector.tensor_scalar(row[:], indf[:, 0, :], float(NKEY), None, ALU.mult)
                dve.drain()
                for o, a, b in ((cand[:, 0, :], val[:, 0, :], val[:, 1, :]), (cand[:, 1, :], row, indf[:, 1, :])):
                    at = 0
                    for r in range(5):
                        n = PAIR_ROWS[r][1]
                        nc.vector.tensor_scalar(o[:, at:at + n], b[:, 0:n], a[:, r:r + 1], None, ALU.add)
                        at += n
                    nc.vector.tensor_tensor(o[:, at:at + 6].rearrange("p (r n) -> p r n", r=3),
                                            a[:, 5:8].unsqueeze(2).broadcast_to([P, 3, 2]),
                                            b[:, 0:2].unsqueeze(1).broadcast_to([P, 3, 2]), ALU.add)
                    nc.vector.tensor_scalar(o[:, at + 6:at + 14], a[:, 8:16], b[:, 0:1], None, ALU.add)
                    assert at + 14 == NCAND
                dve.drain()
                top16([cand[:, 0, :]], [cand_cut[:]], [best], [pos])
                nc.vector.tensor_scalar(soft[:, 0:1], best[:, 0:1], -1.0, None, ALU.mult).then_inc(S["best"], 1)
                nc.vector.tensor_copy(posf[:], pos[:])
                dve.drain()
                full = [P, TOPK, NCAND]
                nc.vector.tensor_tensor(pick[:], iota[:].unsqueeze(1).broadcast_to(full),
                                        posf[:].unsqueeze(2).broadcast_to(full), ALU.is_equal)
                dve.drain()
                nc.vector.tensor_tensor(pick[:], pick[:], cand[:, 1, :].unsqueeze(1).broadcast_to(full), ALU.mult)
                dve.drain()
                nc.vector.tensor_reduce(idxf[:], pick[:], AXX, ALU.add)
                dve.drain()
                nc.vector.tensor_copy(idx_all[:, bass.ds(u * TOPK, TOPK)], idxf[:])
                dve.wait_ge(S["gate_exp"], m + 1)
                nc.vector.reciprocal(soft[:, 2:3], soft[:, 1:2])
                dve.drain()
                nc.vector.tensor_scalar(gate_all[:, bass.ds(u * TOPK, TOPK)], gate[:], soft[:, 2:3], None,
                                        ALU.mult).then_inc(S["routed"], 1)

            route(0, 0, 0)

            def finish(t, rows):
                dve.wait_ge(S["h_in"], t * 16 + 16)
                dve.wait_ge(S["vmm"], t * SLOTS + ((SLOTS if rows == P else 2 * TOPK) + VMM0))
                nc.vector.tensor_tensor(y[0:rows, :], y_acc[0:rows, :], h[0:rows, :], ALU.add)
                dve.drain()
                dve.sem_inc(S["y"], 1)
                dve.wait_ge(S["squares"], t + 1)
                nc.vector.tensor_scalar(stat[0:rows, 1:2], stat[0:rows, 0:1], 1.0 / DM, EPS,
                                        ALU.mult, ALU.add).then_inc(S["mean"], 1)
                dve.wait_ge(S["guess"], t + 1)
                rsqrt_newton(nc, dve, stat[0:rows, 1:2], stat[0:rows, 3:4], stat[0:rows, 4:5], stat[0:rows, 5:6])
                dve.drain()
                nc.vector.scalar_tensor_tensor(y_out[0:rows, :], y[0:rows, :], stat[0:rows, 5:6], g_final[0:rows, :],
                                               ALU.mult, ALU.mult).then_inc(S["y_out"], 1)

            def zero(t, rows):
                dve.drain()
                nc.vector.memset(y_acc[0:rows, :], 0.0).then_inc(S["y_zero"], 1)

            def tile(t, rows):
                if rows < P:
                    for e in range(2):
                        for c in range(COPIES):
                            nc.vector.tensor_copy(shared(idx_sample, e, c), share(idx_all, e, c))
                    dve.drain()
                    dve.sem_inc(S["shared"], 1)
                hold(dve, S["x_ps"], t + 1)

                def unit(u, e, routes, opens):
                    for k in range(TOPK):
                        dve.wait_ge(S_U[k % RING], u * 32 + (k // RING + 1) * 16)
                        slot = u_row[:, k % RING, :]
                        nc.vector.tensor_tensor_reduce(slot, slot, x_ps[:], 1.0, 0.0, ALU.mult, ALU.add,
                                                       hid[:, e, k:k + 1]).then_inc(S["dot"], 1)
                    if opens:
                        finish(t - 1, P)
                        zero(t, rows)
                    hold(dve, S["gelu"], u + 1)
                    if rows == P:
                        nc.vector.tensor_tensor(weight[:, e, :], act_hid[:, e, :],
                                                gate_all[:, bass.ds(u * TOPK, TOPK)], ALU.mult).then_inc(S["weight"], 1)
                    else:
                        for c in range(COPIES):
                            nc.vector.tensor_tensor(shared(weight, e, c), shared(act_hid, e, c),
                                                    share(gate_all, e, c), ALU.mult)
                        dve.drain()
                        dve.sem_inc(S["weight"], 1)
                    for m, of, _, _, bank in routes:
                        route(m, of, bank)
                units(dve, t, rows, unit)
            zero(0, P)
            tiles(dve, tile)
            finish(NT, TS)

        @block.tensor
        def _(pe):
            pe.sem_inc(S["vmm"], VMM0)
            pe.wait_ge(S["const"], 6 * 16)
            for f in range(2):
                last = nc.tensor.transpose(qT_ps[:, f * NKEY:(f + 1) * NKEY], keys[:, f, :], ident[:])
            last.then_inc(S["keys_turn"], 1)
            pe.wait_ge(S["keys_copied"], 1)

            def route(m, x, head, bank):
                pe.wait_ge(S["qe"], m + 1)
                for k in range(DK):
                    last = nc.tensor.matmul(q_ps[:, 0:2 * QH], x[:, k, :], w_q[:, k, bass.ds(head * 2 * QH, 2 * QH)],
                                            start=(k == 0), stop=(k == DK - 1))
                last.then_inc(S["q"], 1)
                pe.wait_ge(S["qe"], m + 2)
                for f in range(2):
                    last = nc.tensor.transpose(qT_ps[:, f * P:(f + 1) * P], q[:, f * QH:(f + 1) * QH], ident[:])
                last.then_inc(S["qt"], 1)
                pe.wait_ge(S["qTe"], m + 1)
                pe.wait_ge(S["routed"], m + 1 - bank)
                for f in range(2):
                    last = nc.tensor.matmul(s_ps[:, bank * 512 + f * NKEY:bank * 512 + (f + 1) * NKEY], qT[:, f, :], keysT[:, f, :],
                                            start=True, stop=True)
                last.then_inc(S["scores"], 1)

            pe.wait_ge(S["xT_first"], 16)
            pe.wait_ge(S["w_q_first"], 16)
            route(0, xT_first, 0, 0)
            pe.wait_ge(S["w_q"], 16)

            def tile(t, rows):
                def unit(u, e, routes, opens):
                    for m, _, x, head, bank in routes:
                        if x is xT:
                            pe.wait_ge(S["xT"], t * 16 + 16)
                        route(m, x, head, bank)
                    hold(pe, S["y_zero"], t + 1)
                    for k in range(TOPK):
                        if k % 4 == 0:
                            pe.wait_ge(S["diag"], u * 4 + (k // 4 + 1))
                        pe.wait_ge(S_V[k % RING], u * 32 + (k // RING + 1) * 16)
                        for b in range(2):
                            last = nc.tensor.matmul(y_acc[0:rows, b * 512:(b + 1) * 512], diag[:, e, k, 0:rows],
                                                    v_row[:, k % RING, b * 512:(b + 1) * 512],
                                                    start=False, stop=True, skip_group_check=True)
                        last.then_inc(S["vmm"], 1)
                units(pe, t, rows, unit)
            tiles(pe, tile)


PHASES = [projection_phase, attention_phase, expert_phase]
OUTPUTS = {
    "y_prompt": (1, SEQ, DM), "y_sample": (1, TS, DM),
    "sb_k_prompt": (1, 1, SEQ, NH, HD), "sb_v_prompt": (1, 1, SEQ, NH, HD),
    "swa_k_prompt": (1, 1, WIN, 2, HD), "swa_v_prompt": (1, 1, WIN, 2, HD),
    "sb_k_sample": (1, 1, TS, NH, HD), "sb_v_sample": (1, 1, TS, NH, HD),
    "swa_k_sample": (1, 1, WIN, 2, HD), "swa_v_sample": (1, 1, WIN, 2, HD),
}
SCRATCH = {
    "projT": (C_END, P, TOK),
    "nat": (TOK, NATW),
    "h": (TOK, DM),
    "xn2": (TOK, DM),
    "xn2T": (NT + 1, P, DK * P),
}
INPUT_SHAPES = {
    "x_prompt": (SEQ, DM), "x_sample": (TS, DM), "cache_sb_k": (PAST, SBW), "cache_sb_v": (PAST, SBW),
    "cache_swa_k": (WIN, KVW), "cache_swa_v": (WIN, KVW), "norm_mix": (1, DM), "w_in": (DM, INW),
    "swa_sinks": (1, NH), "norm_sb_out": (1, SBW), "norm_swa_out": (1, SBW), "w_out": (2 * SBW, DM),
    "norm_ffn": (1, DM), "w_peer_q": (DM, PH * 2 * QH), "peer_keys_1": (NKEY, QH), "peer_keys_2": (NKEY, QH),
    "peer_u": (NKEY * NKEY, DM), "peer_v": (NKEY * NKEY, DM), "norm_final": (1, DM),
}


def lay_out(inputs):
    arrays = {n: np.ascontiguousarray(inputs[n]).reshape(shape) for n, shape in INPUT_SHAPES.items()}
    arrays.update(constants())
    return arrays


def kernel(**inputs):
    import concourse.bacc as _bacc
    from concourse.bass_utils import run_bass_kernel_spmd as _run

    nc = _bacc.Bacc("TRN2", target_bir_lowering=False, num_devices=1)
    arrays = lay_out(inputs)
    io = {n: nc.dram_tensor(n, a.shape, F32, kind="ExternalInput").ap() for n, a in arrays.items()}
    for n, shape in OUTPUTS.items():
        io[n] = nc.dram_tensor(f"out_{n}", shape, F32, kind="ExternalOutput").ap()
    for n, shape in SCRATCH.items():
        io[n] = nc.dram_tensor(f"scratch_{n}", shape, F32, kind="Internal").ap()
    for phase in PHASES:
        phase(nc, io)
    r = _run(nc, [arrays], core_ids=[0])
    return tuple(r.results[0][f"out_{n}"] for n in OUTPUTS)
```
